# Optimizing a Trainium2 kernel written in Bass

```python
import math
import jax, jax.numpy as jnp
from jax import lax
import numpy as np

D_MODEL = 2048
BATCH = 1
SEQ = 256
DEPTH = 2

Q_BLOCK = 128
ROPE_THETA = 500000.0
ROPE_FRACTION_DENOM = 4
NORM_EPS = 1e-6
A_HEADS = 4
A_QK_DIM = 64
A_V_DIM = 128
B_HEADS = 4
B_HEAD_DIM = 128
IDX_HEADS = 8
IDX_DIM = 64
IDX_TOPK_MAX = 256
C_HEADS = 8
C_NOPE_DIM = 128
C_ROPE_DIM = 64
C_QK_DIM = C_NOPE_DIM + C_ROPE_DIM
C_V_DIM = 128
C_KV_RANK = 512
N_BRANCHES = 3
A_OUT = A_HEADS * A_V_DIM
B_OUT = B_HEADS * B_HEAD_DIM
C_OUT = C_HEADS * C_V_DIM
MIX_WIDTH = A_OUT + B_OUT + C_OUT
IN_WIDTHS = (
    A_HEADS * 2 * A_QK_DIM,
    A_HEADS * 2 * A_QK_DIM,
    A_OUT,
    B_HEADS * B_HEAD_DIM,
    B_HEAD_DIM,
    B_HEAD_DIM,
    IDX_HEADS * IDX_DIM,
    IDX_DIM,
    IDX_HEADS,
    C_HEADS * C_QK_DIM,
    C_KV_RANK,
    C_ROPE_DIM,
    N_BRANCHES * D_MODEL,
)
IN_WIDTH = sum(IN_WIDTHS)
D_FF = ((8 * D_MODEL + 3 * 256 - 1) // (3 * 256)) * 256

kernel_name = 'hybrid_gated_diff_dsa_mla_block'

def _rmsnorm(x, g):
    xf = x.astype(jnp.float32)
    y = xf * lax.rsqrt(jnp.mean(xf * xf, axis=-1, keepdims=True) + NORM_EPS)
    return (y * g.astype(jnp.float32)).astype(x.dtype)

def _rope(x, rot_dim):
    seq = x.shape[1]
    half = rot_dim // 2
    pos = jnp.arange(seq, dtype=jnp.float32)
    inv_freq = ROPE_THETA ** (-jnp.arange(half, dtype=jnp.float32) * 2.0 / rot_dim)
    ang = pos[:, None] * inv_freq[None, :]
    cos = jnp.cos(ang)[None, :, None, :]
    sin = jnp.sin(ang)[None, :, None, :]
    xr = x[..., :rot_dim].astype(jnp.float32)
    x1, x2 = xr[..., :half], xr[..., half:]
    rot = jnp.concatenate([x1 * cos - x2 * sin, x2 * cos + x1 * sin], axis=-1).astype(x.dtype)
    return jnp.concatenate([rot, x[..., rot_dim:]], axis=-1)

def _split_cols(t, widths):
    cuts, acc = [], 0
    for w in widths[:-1]:
        acc += w
        cuts.append(acc)
    return jnp.split(t, cuts, axis=-1)

def _masked_softmax(s, scale, mask):
    s = jnp.where(mask, s.astype(jnp.float32) * scale, -jnp.inf)
    return jax.nn.softmax(s, axis=-1)

def _causal_mask(start, seq):
    qpos = start + jnp.arange(Q_BLOCK, dtype=jnp.int32)
    mask = jnp.arange(seq, dtype=jnp.int32)[None, :] <= qpos[:, None]
    return qpos, mask

def _sweep_query_blocks(block_fn, seq):
    starts = jnp.arange(seq // Q_BLOCK, dtype=jnp.int32) * Q_BLOCK
    out = lax.map(block_fn, starts)
    out = jnp.moveaxis(out, 0, 1)
    return out.reshape(out.shape[:1] + (seq,) + out.shape[3:])

def _diff_attention(q1, q2, k1, k2, v, lam):
    seq = q1.shape[1]
    scale = A_QK_DIM ** -0.5

    def block(start):
        _, mask = _causal_mask(start, seq)
        q1b = lax.dynamic_slice_in_dim(q1, start, Q_BLOCK, axis=1)
        q2b = lax.dynamic_slice_in_dim(q2, start, Q_BLOCK, axis=1)
        p1 = _masked_softmax(jnp.einsum('bqhd,bkhd->bhqk', q1b, k1), scale, mask)
        p2 = _masked_softmax(jnp.einsum('bqhd,bkhd->bhqk', q2b, k2), scale, mask)
        p = (p1 - lam * p2).astype(v.dtype)
        return jnp.einsum('bhqk,bkhd->bqhd', p, v)

    return _sweep_query_blocks(block, seq)

def _dense_attention(q, k, v, scale):
    seq = q.shape[1]

    def block(start):
        _, mask = _causal_mask(start, seq)
        qb = lax.dynamic_slice_in_dim(q, start, Q_BLOCK, axis=1)
        p = _masked_softmax(jnp.einsum('bqhd,bkhd->bhqk', qb, k), scale, mask)
        return jnp.einsum('bhqk,bkhd->bqhd', p.astype(v.dtype), v)

    return _sweep_query_blocks(block, seq)

def _dsa_attention(q, k, v, q_idx, k_idx, w_idx):
    seq = k.shape[1]
    top_k = min(IDX_TOPK_MAX, seq // 4)
    scale = B_HEAD_DIM ** -0.5
    gather = jax.vmap(lambda t, i: t[i])

    def block(start):
        qpos, mask = _causal_mask(start, seq)
        qib = lax.dynamic_slice_in_dim(q_idx, start, Q_BLOCK, axis=1)
        wb = lax.dynamic_slice_in_dim(w_idx, start, Q_BLOCK, axis=1)
        rel = jax.nn.relu(jnp.einsum('bqhd,bkd->bqhk', qib, k_idx).astype(jnp.float32))
        score = jnp.einsum('bqh,bqhk->bqk', wb.astype(jnp.float32), rel)
        score = jnp.where(mask, score, -jnp.inf)
        _, sel = lax.top_k(score, top_k)
        valid = sel <= qpos[None, :, None]
        kg = gather(k, sel)
        vg = gather(v, sel)
        qb = lax.dynamic_slice_in_dim(q, start, Q_BLOCK, axis=1)
        p = _masked_softmax(jnp.einsum('bqhd,bqkd->bqhk', qb, kg), scale, valid[:, :, None, :])
        return jnp.einsum('bqhk,bqkd->bqhd', p.astype(vg.dtype), vg)

    return _sweep_query_blocks(block, seq)

def _hybrid_mixer(h, lam_init, w_in, a_q_norm, a_k_norm, a_lambda, a_sub_norm, b_q_norm, b_k_norm,
                  idx_k_norm, c_q_norm, c_kv_norm, w_kv_b, c_k_norm, w_branch, w_out):
    bsz, seq, _ = h.shape
    (a_q, a_k, a_v, b_q, b_k, b_v, i_q, i_k, i_w, c_q, c_kv, c_kr, gates) = _split_cols(h @ w_in, IN_WIDTHS)

    a_rot = A_QK_DIM // ROPE_FRACTION_DENOM
    aq = _rope(_rmsnorm(a_q.reshape(bsz, seq, 2 * A_HEADS, A_QK_DIM), a_q_norm), a_rot)
    ak = _rope(_rmsnorm(a_k.reshape(bsz, seq, 2 * A_HEADS, A_QK_DIM), a_k_norm), a_rot)
    aq = aq.reshape(bsz, seq, A_HEADS, 2, A_QK_DIM)
    ak = ak.reshape(bsz, seq, A_HEADS, 2, A_QK_DIM)
    av = a_v.reshape(bsz, seq, A_HEADS, A_V_DIM)
    lf = a_lambda.astype(jnp.float32)
    lam = jnp.exp(jnp.sum(lf[0] * lf[1])) - jnp.exp(jnp.sum(lf[2] * lf[3])) + lam_init
    a_o = _diff_attention(aq[..., 0, :], aq[..., 1, :], ak[..., 0, :], ak[..., 1, :], av, lam)
    a_o = (_rmsnorm(a_o, a_sub_norm) * (1.0 - lam_init)).reshape(bsz, seq, A_OUT)

    b_rot = B_HEAD_DIM // ROPE_FRACTION_DENOM
    i_rot = IDX_DIM // ROPE_FRACTION_DENOM
    bq = _rope(_rmsnorm(b_q.reshape(bsz, seq, B_HEADS, B_HEAD_DIM), b_q_norm), b_rot)
    bk = _rope(_rmsnorm(b_k.reshape(bsz, seq, 1, B_HEAD_DIM), b_k_norm), b_rot)[:, :, 0]
    iq = _rope(i_q.reshape(bsz, seq, IDX_HEADS, IDX_DIM), i_rot)
    ik = _rope(_rmsnorm(i_k, idx_k_norm)[:, :, None, :], i_rot)[:, :, 0]
    iw = i_w * (IDX_HEADS ** -0.5 * IDX_DIM ** -0.5)
    b_o = _dsa_attention(bq, bk, b_v, iq, ik, iw).reshape(bsz, seq, B_OUT)

    cq = _rope(_rmsnorm(c_q.reshape(bsz, seq, C_HEADS, C_QK_DIM), c_q_norm), C_ROPE_DIM)
    kv = (_rmsnorm(c_kv, c_kv_norm) @ w_kv_b).reshape(bsz, seq, C_HEADS, C_NOPE_DIM + C_V_DIM)
    k_nope, c_v = kv[..., :C_NOPE_DIM], kv[..., C_NOPE_DIM:]
    k_rope = jnp.broadcast_to(c_kr[:, :, None, :], (bsz, seq, C_HEADS, C_ROPE_DIM))
    ck = _rope(_rmsnorm(jnp.concatenate([k_rope, k_nope], axis=-1), c_k_norm), C_ROPE_DIM)
    c_o = _dense_attention(cq, ck, c_v, C_QK_DIM ** -0.5).reshape(bsz, seq, C_OUT)

    g = jax.nn.sigmoid(gates.reshape(bsz, seq, N_BRANCHES, D_MODEL).astype(jnp.float32)).astype(h.dtype)
    w_a = w_branch[:A_OUT]
    w_b = w_branch[A_OUT:A_OUT + B_OUT]
    w_c = w_branch[A_OUT + B_OUT:]
    merged = g[:, :, 0] * (a_o @ w_a) + g[:, :, 1] * (b_o @ w_b) + g[:, :, 2] * (c_o @ w_c)
    return merged @ w_out

def setup_inputs(seed: int = 0) -> dict:
    key = jax.random.key(seed)
    ks = jax.random.split(key, 20)

    def nrm(k, shape, scale):
        return jax.random.normal(k, shape, jnp.float32) * scale

    def gain(k, n):
        return 1.0 + 0.02 * jax.random.normal(k, (DEPTH, n), jnp.float32)

    return {
        'x': nrm(ks[0], (BATCH, SEQ, D_MODEL), 1.0),
        'attn_norm': gain(ks[1], D_MODEL),
        'w_in': nrm(ks[2], (DEPTH, D_MODEL, IN_WIDTH), D_MODEL ** -0.5),
        'a_q_norm': gain(ks[3], A_QK_DIM),
        'a_k_norm': gain(ks[4], A_QK_DIM),
        'a_lambda': nrm(ks[5], (DEPTH, 4, A_QK_DIM), 0.1),
        'a_sub_norm': gain(ks[6], A_V_DIM),
        'b_q_norm': gain(ks[7], B_HEAD_DIM),
        'b_k_norm': gain(ks[8], B_HEAD_DIM),
        'idx_k_norm': gain(ks[9], IDX_DIM),
        'c_q_norm': gain(ks[10], C_QK_DIM),
        'c_kv_norm': gain(ks[11], C_KV_RANK),
        'w_kv_b': nrm(ks[12], (DEPTH, C_KV_RANK, C_HEADS * (C_NOPE_DIM + C_V_DIM)), C_KV_RANK ** -0.5),
        'c_k_norm': gain(ks[13], C_QK_DIM),
        'w_branch': nrm(ks[14], (DEPTH, MIX_WIDTH, D_MODEL), MIX_WIDTH ** -0.5),
        'w_out': nrm(ks[15], (DEPTH, D_MODEL, D_MODEL), D_MODEL ** -0.5),
        'ffn_norm': gain(ks[16], D_MODEL),
        'w_gate_up': nrm(ks[17], (DEPTH, D_MODEL, 2 * D_FF), D_MODEL ** -0.5),
        'w_down': nrm(ks[18], (DEPTH, D_FF, D_MODEL), D_FF ** -0.5),
    }

def reference(x, attn_norm, w_in, a_q_norm, a_k_norm, a_lambda, a_sub_norm, b_q_norm, b_k_norm,
              idx_k_norm, c_q_norm, c_kv_norm, w_kv_b, c_k_norm, w_branch, w_out, ffn_norm,
              w_gate_up, w_down):
    for l in range(DEPTH):
        lam_init = 0.8 - 0.6 * math.exp(-0.3 * l)
        h = _rmsnorm(x, attn_norm[l])
        x = x + _hybrid_mixer(h, lam_init, w_in[l], a_q_norm[l], a_k_norm[l], a_lambda[l], a_sub_norm[l],
                              b_q_norm[l], b_k_norm[l], idx_k_norm[l], c_q_norm[l], c_kv_norm[l],
                              w_kv_b[l], c_k_norm[l], w_branch[l], w_out[l])
        h = _rmsnorm(x, ffn_norm[l])
        gate, up = jnp.split(h @ w_gate_up[l], 2, axis=-1)
        x = x + (jax.nn.silu(gate) * up) @ w_down[l]
    return x


_drawn_inputs = setup_inputs


def setup_inputs(seed=0):
    import zlib

    import numpy as np

    out = dict(_drawn_inputs(seed))
    spreads = {}
    factors = {'attn_norm': 3.419,
     'a_q_norm': 8.0,
     'a_k_norm': 8.0,
     'a_sub_norm': 7.711,
     'b_q_norm': 8.0,
     'b_k_norm': 8.0,
     'idx_k_norm': 6.831,
     'c_q_norm': 8.0,
     'c_kv_norm': 8.0,
     'c_k_norm': 8.0,
     'ffn_norm': 2.701}
    for name, (base, spread) in spreads.items():
        noise = np.random.default_rng([zlib.crc32(name.encode()), seed]).standard_normal(out[name].shape)
        drawn = base * np.exp(spread * noise) if base else spread * noise
        out[name] = __import__('jax').numpy.asarray(drawn.astype(out[name].dtype))
    for name, factor in factors.items():
        out[name] = (out[name] * factor).astype(out[name].dtype)
    return out
```

```python
import math
from contextlib import ExitStack, contextmanager

import numpy as np

import concourse.bass as bass
from concourse import mybir
from concourse.alu_op_type import AluOpType as ALU

F32 = mybir.dt.float32
F32R = mybir.dt.float32r
ACT = mybir.ActivationFunctionType
AX = mybir.AxisListType.X
ds = bass.ds

P = 128
SEQ, D, DEPTH = 256, 2048, 2
NT = SEQ // P
KT = D // P
A_HEADS, A_QK, A_V = 4, 64, 128
B_HEADS, B_DIM = 4, 128
I_HEADS, I_DIM = 8, 64
C_HEADS, C_NOPE, C_ROPE, C_V, C_RANK = 8, 128, 64, 128, 512
C_QK = C_NOPE + C_ROPE
TOPK = min(256, SEQ // 4)
THETA = 500000.0
EPS = 1e-6
D_FF = ((8 * D + 3 * 256 - 1) // (3 * 256)) * 256

W_COLS = [2 * A_HEADS * A_QK, 2 * A_HEADS * A_QK, A_HEADS * A_V, B_HEADS * B_DIM, B_DIM, B_DIM,
          I_HEADS * I_DIM, I_DIM, I_HEADS, C_HEADS * C_QK, C_RANK, C_ROPE]
AQ, AK, AV, BQ, BK, BV, IQ, IK, IW, CQ, CKV, CKR, GATES = [sum(W_COLS[:n]) for n in range(len(W_COLS) + 1)]

N = 512
KU = 2
RING = 4
UB = 8
PC = GATES // 10
PROJ1, PROJ2 = 6, 4
NG = 3 * D // N
NC = D // N
NF = D_FF // N
B_A = PROJ1 + PROJ2
B_KV = B_A + A_HEADS
B_C = B_KV + 1
B_BR = B_C + C_HEADS
B_OUT = B_BR + NC
B_FF = B_OUT + NC
B_DN = B_FF + 2 * NF
BLOCKS = B_DN + NF
assert PC * 10 == GATES and PC <= N and C_HEADS + A_HEADS == NG and NF % 2 == 1

G_A, G_KV, G_C, ACT_GROUPS = B_A, B_A + A_HEADS, B_A + A_HEADS + NC, B_A + NG + NC
V_OUT, V_FF, V_DN, DVE_GROUPS = 3 * NC, 4 * NC, 4 * NC + 2 * NF, 5 * NC + 2 * NF
CREDIT = 3

KEYS = 3 * P
SEG = [(0, P), (P, 3 * P)]
NEG = -3e38
TAKEN = float(np.float32(-3.4e38))

ROT = {"a": A_QK // 4, "b": B_DIM // 4, "c": C_ROPE}
ROPE_AT = {"a": 0, "b": 2 * ROT["a"], "c": 2 * (ROT["a"] + ROT["b"])}
ROPE_W = 2 * sum(ROT.values())

GAINS = [("a_q_norm", A_QK), ("a_q_norm", A_QK), ("a_k_norm", A_QK), ("a_k_norm", A_QK), ("a_sub_norm", A_V),
         ("b_q_norm", B_DIM), ("b_k_norm", B_DIM), ("idx_k_norm", I_DIM), ("c_q_norm", C_QK), ("c_k_norm", C_QK)]
GA, _, _, _, GSUB, GBQ, GBK, GIK, GCQ, GCK, G_W = [sum(w for _, w in GAINS[:n]) for n in range(len(GAINS) + 1)]


def rope_table():
    pos = np.arange(SEQ, dtype=np.float32)
    out = []
    for rot in ROT.values():
        half = rot // 2
        inv = (np.float32(THETA) ** (-np.arange(half, dtype=np.float32) * np.float32(2.0) / np.float32(rot)))
        ang = pos[:, None] * inv.astype(np.float32)[None, :]
        out += [np.cos(ang), np.cos(ang), -np.sin(ang), np.sin(ang)]
    return np.concatenate(out, axis=1).astype(np.float32)


class Steps:

    def __init__(self, eng, sem, mark):
        self.eng, self.sem, self.mark, self.base, self.n = eng, sem, mark, 0, 0

    def hold(self):
        self.eng.sem_inc(self.mark, 1)

    def __call__(self, ins, wait=True):
        self.n += 1
        ins.then_inc(self.sem, 1)
        if wait:
            self.eng.wait_ge(self.sem, self.base + self.n)

    @contextmanager
    def turn(self, i, count, stride):
        base, n = self.base, self.n
        self.base, self.n = base + n + i * stride, 0
        yield
        assert 0 < self.n < stride, (self.n, stride)
        self.eng.sem_inc(self.sem, stride - self.n)
        self.base, self.n = base, n + count * stride


def hybrid_trunk(nc, x, attn_norm, w_in, a_q_norm, a_k_norm, a_lambda, a_sub_norm, b_q_norm, b_k_norm,
                 idx_k_norm, c_q_norm, c_kv_norm, w_kv_b, c_k_norm, w_branch, w_out, ffn_norm,
                 w_gate_up, w_down, rope_tab, out):
    gain_of = dict(a_q_norm=a_q_norm, a_k_norm=a_k_norm, a_sub_norm=a_sub_norm, b_q_norm=b_q_norm,
                   b_k_norm=b_k_norm, idx_k_norm=idx_k_norm, c_q_norm=c_q_norm, c_k_norm=c_k_norm)
    gate_store = nc.dram_tensor("gate_store", (DEPTH * NG, P, NT * N), F32, kind="Internal").ap()

    with ExitStack() as ctx:
        def sb(name, shape, dt=F32):
            return ctx.enter_context(nc.sbuf_tensor(name, shape, dt))

        def sem(name):
            return ctx.enter_context(nc.semaphore(name))

        acc = ctx.enter_context(nc.psum_tensor("acc", [P, 8, 512], F32))

        xs = sb("xs", [P, NT, D])
        opa = [sb("opa_hi", [P, KT, SEQ], F32R), sb("opa_lo", [P, KT, SEQ], F32R)]
        opb = [sb("opb_hi", [P, KT, SEQ], F32R), sb("opb_lo", [P, KT, SEQ], F32R)]
        raw = sb("w_raw", [P, RING, KU, N])
        w_hi = sb("w_hi", [P, RING, KU, N], F32R)
        w_lo = sb("w_lo", [P, RING, KU, N], F32R)
        arena = sb("arena", [P, NT * (GATES + C_HEADS * (C_NOPE + C_V))])
        nat = sb("nat", [P, NT, N])
        tmp = sb("tmp", [P, 1024])
        small = sb("small", [P, 4096])
        score_i = sb("score_i", [P, KEYS])
        rope_sb = sb("rope_sb", [P, NT, ROPE_W])
        gains = sb("gains", [P, G_W])
        ident = sb("ident", [P, P])
        causal = sb("causal", [P, KEYS])
        gcol = sb("gcol", [P, 72])
        gnow = sb("gnow", [P, 2 * KT + 4])
        stats = sb("stats", [P, 48])
        xsq = sb("xsq", [P, NT, NC])
        rs = sb("rs", [P, 96])
        rx = sb("rx", [P, 4])
        root_sb = sb("root_sb", [P, 48])
        lam = sb("lam", [P, 8])
        laminit = sb("laminit", [P, DEPTH, 2])
        iws = sb("iws", [P, NT, I_HEADS])
        top8 = sb("top8", [P, NT, 8])
        nmax = sb("nmax", [P, 2, NT])
        sums = sb("sums", [P, 2, NT])
        rsum = sb("rsum", [P, 2, NT])
        krot = sb("krot", [P, NT, C_ROPE])
        rck = sb("rck", [P, NT, C_HEADS])

        proj = arena[:, 0:NT * GATES].rearrange("p (t n) -> p t n", t=NT)
        kv = arena[:, NT * GATES:].rearrange("p (t h n) -> p t h n", t=NT, h=C_HEADS)
        kv_rows = arena[:, NT * GATES:].rearrange("p (t n) -> p t n", t=NT)
        gates = arena[:, A_HEADS * A_V:A_HEADS * A_V + 13 * NT * N].rearrange("p (k n) -> p k n", n=NT * N)
        BRANCH_ORDER = (1, 0, 2)
        FIRST_PIECES = (0, 5, 1)
        hid_t = arena[:, 0:4 * NF * SEQ].rearrange("p (k s) -> p k s", k=4 * NF)
        lamb = small[:, 3840:4096].rearrange("p (f d) -> p f d", f=4)

        def part(a, n):
            return small[:, a:a + n]

        q_rows = part(0, NT * C_QK).rearrange("p (t n) -> p t n", t=NT)
        k_rows = part(384, NT * C_QK).rearrange("p (t n) -> p t n", t=NT)
        v_rows = part(768, NT * C_V).rearrange("p (t n) -> p t n", t=NT)
        qk_rows = part(0, 2 * NT * P).rearrange("p (m t n) -> p m t n", m=2, t=NT)
        bq_rows = part(1024, NT * P).rearrange("p (t n) -> p t n", t=NT)
        ik_rows = part(768, NT * P).rearrange("p (t n) -> p t n", t=NT)
        q_t = small[:, 1280:1792]
        k_t = small[:, 1792:2304]
        s_sb = part(2304, 2 * KEYS).rearrange("p (m n) -> p m n", m=2)
        e_sb = part(3072, 2 * KEYS).rearrange("p (m n) -> p m n", m=2)
        bk_t = sb("bk_t", [P, SEQ])
        bq_t = tmp[:, 768:1024]
        p_t = sb("p_t", [P, 2, KEYS])
        t_row = part(0, NT * N).rearrange("p (t n) -> p t n", t=NT)
        sg = part(1024, NT * N).rearrange("p (t n) -> p t n", t=NT)
        gg = part(2048, NT * N).rearrange("p (t n) -> p t n", t=NT)

        raw_landed = [sem(f"raw_landed{s}") for s in range(RING)]
        hi_ready, lo_ready, unit_done = sem("hi_ready"), sem("lo_ready"), sem("unit_done")
        act_emptied, dve_emptied = sem("act_emptied"), sem("dve_emptied")
        const_landed, gains_landed, stored = sem("const_landed"), sem("gains_landed"), sem("stored")
        x_landed = [sem(f"x_landed{j}") for j in range(NC)]
        rope_landed, x_now = sem("rope_landed"), sem("x_now")
        pool_const, gcol_t, gains_free = sem("pool_const"), sem("gcol_t"), sem("gains_free")
        dve_step, dve_mark = sem("dve_step"), sem("dve_mark")
        var_ready, root_ready = sem("var_ready"), sem("root_ready")
        rx_ready, rs_ready = sem("rx_ready"), sem("rs_ready")
        gnow_ready = sem("gnow_ready")
        x_t, x_hi, x_lo = sem("x_t"), sem("x_hi"), sem("x_lo")
        m_rows, m_t, m_hi, m_lo = sem("m_rows"), sem("m_t"), sem("m_hi"), sem("m_lo")
        ckv_t, ckv_hi, ckv_lo = sem("ckv_t"), sem("ckv_hi"), sem("ckv_lo")
        ao_rows, ao_t, ao_hi, ao_lo = sem("ao_rows"), sem("ao_t"), sem("ao_hi"), sem("ao_lo")
        i_staged, i_t, i_sb, i_scored, i_relu, i_summed = (sem("i_staged"), sem("i_t"), sem("i_sb"),
                                                           sem("i_scored"), sem("i_relu"), sem("i_summed"))
        lam_dots, lam_exp = sem("lam_dots"), sem("lam_exp")
        head = {h: {n: sem(f"{h}_{n}") for n in ("staged", "qk_t", "qk_sb", "scored", "maxed", "exped", "p_ready",
                                                  "p_t", "p_sb", "o_done", "o_hi", "o_out")} for h in "abc"}
        gate_saved = sem("gate_saved")
        gate_back = [sem(f"gate_back{r}") for r in range(3)]
        gate_open = sem("gate_open")
        sig_ready, h_t, h_sb, jit_hi, jit_lo = (sem("sig_ready"), sem("h_t"), sem("h_sb"), sem("jit_hi"), sem("jit_lo"))

        block = ctx.enter_context(nc.Block())

        def units(l, blk):
            return l * (BLOCKS * UB) + blk * UB

        def bank(pair, t=None, n=N):
            return acc[:, 2 * pair:2 * pair + 2, 0:n] if t is None else acc[:, 2 * pair + t, 0:n]

        @block.sync
        def _(sp):
            def weights(w, k_units):
                return w.rearrange("l (u k p) n -> p (l u) k n", k=KU, p=P), k_units

            win, wkv, wbr, wout, wgu, wdn = (weights(w_in, UB), weights(w_kv_b, 2), weights(w_branch, UB),
                                             weights(w_out, UB), weights(w_gate_up, UB), weights(w_down, 2 * NF))

            def unit(n, m, w, l, u, col, width=N):
                slot = m % RING
                sp.wait_ge(lo_ready, n + (m + 1))
                view, per = w
                sp.dma_start(raw[:, slot:slot + 1, :, 0:width],
                             view[:, ds(l * per + u, 1), :, ds(col, width)]).then_inc(raw_landed[slot], 16)

            row = 0
            for g in (attn_norm, ffn_norm, c_kv_norm):
                rows = g.rearrange("l (k p) -> (l k) p", p=P)
                sp.dma_start(small[row:row + rows.shape[0], 0:P], rows).then_inc(const_landed, 16)
                row += rows.shape[0]
            x_rows = x.rearrange("a (t p) n -> p (a t) n", p=P)
            for j in range(NC):
                sp.dma_start(xs[:, :, j * N:(j + 1) * N], x_rows[:, :, j * N:(j + 1) * N]).then_inc(x_landed[j], 16)

            with sp.Fori(0, DEPTH) as l:
                with sp.Fori(0, PROJ1) as c:
                    n = sp.snap(units(l, 0) + c * UB)
                    for m in range(UB):
                        unit(n, m, win, l, m, c * PC, PC)
                with sp.Fori(0, PROJ2) as c:
                    n = sp.snap(units(l, PROJ1) + c * UB)
                    for m in range(UB):
                        unit(n, m, win, l, m, (PROJ1 + PROJ2 - 1) * PC - c * PC, PC)
                with sp.Fori(0, A_HEADS) as c:
                    n = sp.snap(units(l, B_A) + c * UB)
                    for m in range(UB):
                        unit(n, m, win, l, m, GATES + c * N)
                for m in range(UB):
                    unit(units(l, B_KV), m, wkv, l, m % 2, (m // 2) * N)
                with sp.Fori(0, C_HEADS) as c:
                    n = sp.snap(units(l, B_C) + c * UB)
                    for m in range(UB):
                        unit(n, m, win, l, m, GATES + A_HEADS * N + c * N)
                with sp.Fori(0, NC) as c:
                    n = sp.snap(units(l, B_BR) + c * UB)
                    for m, u in enumerate((2, 3, 0, 1, 4, 5, 6, 7)):
                        unit(n, m, wbr, l, u, c * N)
                with sp.Fori(0, NC) as c:
                    n = sp.snap(units(l, B_OUT) + c * UB)
                    for m in range(UB):
                        unit(n, m, wout, l, m, c * N)
                with sp.Fori(0, NF) as c:
                    n = sp.snap(units(l, B_FF) + c * (2 * UB))
                    for m in range(2 * UB):
                        unit(n, m, wgu, l, m % UB, c * N + (m // UB) * D_FF)
                with sp.Fori(0, NF) as c:
                    n = sp.snap(units(l, B_DN) + c * UB)
                    for m in range(UB):
                        unit(n, m, wdn, l, c * 2 + m % 2, (m // 2) * N)

            sp.wait_ge(dve_emptied, CREDIT + DEPTH * DVE_GROUPS)
            sp.dma_start(out.rearrange("a (t p) n -> p (a t) n", p=P), xs[:, :, :]).then_inc(stored, 16)
            sp.wait_ge(stored, 16)

        @block.gpsimd
        def _(pool):
            pool.memset(ident[:, :], 0.0).then_inc(pool_const, 1)
            pool.memset(causal[:, :], 0.0).then_inc(pool_const, 1)
            pool.memset(raw[:, :, :, PC:N], 0.0).then_inc(pool_const, 1)
            pool.sem_inc(lo_ready, RING)
            pool.wait_ge(pool_const, 3)
            pool.affine_select(out=ident[:, :], in_=ident[:, :], compare_op=ALU.not_equal, fill=1.0, base=0,
                               pattern=[[-1, P]], channel_multiplier=1).then_inc(pool_const, 1)
            for b in (0, 2):
                d = causal[:, b * P:(b + 1) * P]
                pool.affine_select(out=d, in_=d, compare_op=ALU.is_ge, fill=NEG, base=0,
                                   pattern=[[-1, P]], channel_multiplier=1).then_inc(pool_const, 1)
            with pool.Fori(0, DEPTH * BLOCKS) as b:
                n = pool.snap(b * UB)
                for m in range(UB):
                    s = m % RING
                    pool.wait_ge(hi_ready, n + (m + 1))
                    pool.tensor_tensor(w_lo[:, s], raw[:, s], w_hi[:, s].bitcast(F32), ALU.subtract).then_inc(lo_ready, 1)

        @block.tensor
        def _(pe):
            def unit(n, m, op, kt, pair, first, last, width=N):
                s = m % RING
                pe.wait_ge(lo_ready, n + (RING + m + 1))
                passes = [(op[0], w_hi), (op[0], w_lo), (op[1], w_hi)]
                for k in range(KU):
                    for t in range(NT):
                        for j, (a, w) in enumerate(passes):
                            mm = pe.matmul(bank(pair, t, width), a[:, kt + k, t * P:(t + 1) * P], w[:, s, k, 0:width],
                                           start=(first and k == 0 and j == 0), stop=(last and k == KU - 1 and j == 2))
                mm.then_inc(unit_done, 1)

            def whole(n, m0, op, pair, after, width=N, need=None):
                for m in range(UB):
                    if need:
                        need(m)
                    unit(n, m0 + m, op, KU * m, pair, m == 0, m == UB - 1, width)
                    if m in after:
                        after[m]()

            def rows_to_cols(b0, rows, tiles=4):
                for k in range(tiles):
                    for t in range(NT):
                        at = k * SEQ + t * P
                        mm = pe.transpose(acc[:, b0 + at // 512, at % 512:at % 512 + P],
                                          rows[:, t, k * P:(k + 1) * P], ident[:, :])
                return mm

            def scores(out, q, k, done):
                for j in range(len(q)):
                    pe.matmul(out[:, 0:P], q[j][:, 0:P], k[j][:, 0:P], start=(j == 0), stop=(j == len(q) - 1))
                for j in range(len(q)):
                    mm = pe.matmul(out[:, P:KEYS], q[j][:, P:SEQ], k[j], start=(j == 0), stop=(j == len(q) - 1))
                if done is not None:
                    mm.then_inc(done, 1)

            def probs_t(b, e, done):
                for j in range(3):
                    mm = pe.transpose(acc[:, b, j * P:(j + 1) * P], e[:, j * P:(j + 1) * P], ident[:, :])
                mm.then_inc(done, 1)

            def out_t(b, v, pt, done):
                pe.matmul(acc[:, b, 0:SEQ], v[:, 0], pt[:, 0:SEQ], start=True, stop=False)
                pe.matmul(acc[:, b, P:SEQ], v[:, 1], pt[:, SEQ:KEYS], start=False, stop=True).then_inc(done, 1)

            pe.wait_ge(pool_const, 6)
            pe.wait_ge(const_landed, 16 * 3)
            pe.transpose(acc[:, 7, 0:72], small[0:72, 0:P], ident[0:72, 0:72]).then_inc(gcol_t, 1)
            pe.sem_inc(unit_done, RING)

            with pe.Fori(0, DEPTH) as l:
                for j in range(NC):
                    pe.wait_ge(x_now, l * NC + (j + 1))
                    if j == NC - 1:
                        pe.wait_ge(gnow_ready, 1)
                    rows_to_cols(2 * j, xs[:, :, j * N:(j + 1) * N]).then_inc(x_t, 1)

                def need_x(m):
                    if m % 2 == 0:
                        pe.wait_ge(x_lo, l * (2 * NC) + (m // 2 + 1))

                with pe.Fori(0, PROJ1 // 2) as i:
                    n = pe.snap(units(l, 0) + i * (2 * UB))
                    g = pe.snap(l * ACT_GROUPS + i * 2)
                    for e in range(2):
                        pe.wait_ge(act_emptied, g + (e + 1))
                        whole(n, e * UB, opa, e, {}, PC, need_x)

                with pe.Fori(0, PROJ2 // 2) as i:
                    n = pe.snap(units(l, PROJ1) + i * (2 * UB))
                    g = pe.snap(l * ACT_GROUPS + PROJ1 + i * 2)
                    h = pe.snap(l * PROJ2 + i * 2)
                    for e in range(2):
                        pe.wait_ge(act_emptied, g + (e + 1))

                        def pair_t():
                            pe.wait_ge(i_staged, h + (e + 1))
                            for t in range(NT):
                                pe.transpose(acc[:, 4, t * P:(t + 1) * P], bq_rows[:, t], ident[:, :])
                                pe.transpose(acc[:, 4, SEQ + t * P:SEQ + (t + 1) * P], ik_rows[:, t], ident[:, :])
                                mm = pe.transpose(acc[:, 5, t * P:(t + 1) * P], proj[:, t, BK:BK + P], ident[:, :])
                            mm.then_inc(i_t, 1)

                        def pair_scores():
                            pe.wait_ge(i_sb, h + (e + 1))
                            for m in range(2):
                                r = slice(64 * m, 64 * m + 64)
                                scores(acc[:, 6 + m, 0:KEYS], [q_t[r, 0:SEQ]], [q_t[r, SEQ:2 * SEQ]],
                                       i_scored if m else None)

                        whole(n, e * UB, opa, e, {4: pair_t, 5: pair_scores}, PC)

                pe.wait_ge(act_emptied, l * ACT_GROUPS + (2 + PROJ1 + 2))
                rows_to_cols(4, proj[:, :, CKV:CKV + C_RANK]).then_inc(ckv_t, 1)

                A = head["a"]
                with pe.Fori(0, A_HEADS // 2) as i:
                    n = pe.snap(units(l, B_A) + i * (2 * UB))
                    g = pe.snap(l * ACT_GROUPS + G_A + i * 2)
                    h = pe.snap(l * A_HEADS + i * 2)
                    for e in range(2):
                        pe.wait_ge(act_emptied, g + (e + 1))

                        def a_t():
                            pe.wait_ge(A["staged"], h + (e + 1))
                            pe.wait_ge(ckv_lo, l + 1)
                            for m in range(2):
                                for t in range(NT):
                                    mm = pe.transpose(acc[:, 4, m * SEQ + t * P:m * SEQ + (t + 1) * P],
                                                      qk_rows[:, m, t], ident[:, :])
                            mm.then_inc(A["qk_t"], 1)

                        def a_scores():
                            pe.wait_ge(A["qk_sb"], h + (e + 1))
                            for m in range(2):
                                r = slice(64 * m, 64 * m + 64)
                                scores(acc[:, 5 + m, 0:KEYS], [q_t[r, 0:SEQ]], [q_t[r, SEQ:2 * SEQ]],
                                       A["scored"] if m else None)

                        def a_p_t():
                            pe.wait_ge(A["p_ready"], h + (e + 1))
                            probs_t(4, e_sb[:, 0], A["p_t"])

                        def a_out():
                            pe.wait_ge(A["p_sb"], h + (e + 1))
                            pe.wait_ge(A["o_out"], h + (e + 1))
                            pt = p_t[:, 0]
                            pe.matmul(acc[:, 7, 0:P], pt[:, 0:P], v_rows[:, 0], start=True, stop=True)
                            pe.matmul(acc[:, 7, P:SEQ], pt[:, P:SEQ], v_rows[:, 0], start=True, stop=False)
                            pe.matmul(acc[:, 7, P:SEQ], pt[:, SEQ:KEYS], v_rows[:, 1], start=False,
                                      stop=True).then_inc(A["o_done"], 1)

                        whole(n, e * UB, opa, e, {1: a_t, 2: a_scores, 5: a_p_t, 6: a_out})

                n = units(l, B_KV)
                for j in range(NC):
                    pe.wait_ge(act_emptied, l * ACT_GROUPS + (G_KV + j + 1))
                    if j == NC - 1:
                        pe.wait_ge(A["o_out"], (l + 1) * A_HEADS + 1)
                    for u in range(2):
                        unit(n, 2 * j + u, opb, KU * u, j % 2, u == 0, u == 1)

                B, C = head["b"], head["c"]
                with pe.Fori(0, C_HEADS // 2) as i:
                    n = pe.snap(units(l, B_C) + i * (2 * UB))
                    g = pe.snap(l * ACT_GROUPS + G_C + i * 2)
                    h = pe.snap(l * C_HEADS + i * 2)
                    hb = pe.snap(l * B_HEADS + i)
                    for e in range(2):
                        pe.wait_ge(act_emptied, g + (e + 1))

                        def c_t():
                            pe.wait_ge(C["staged"], h + (e + 1))
                            if e == 1:
                                pe.wait_ge(B["p_ready"], hb + 1)
                            half = C_QK // 2
                            for b, rows in ((4, q_rows), (5, k_rows)):
                                for j in range(2):
                                    for t in range(NT):
                                        mm = pe.transpose(acc[0:half, b, j * SEQ + t * P:j * SEQ + (t + 1) * P],
                                                          rows[:, t, j * half:(j + 1) * half], ident[:, :])
                            mm.then_inc(C["qk_t"], 1)

                        def c_scores():
                            pe.wait_ge(C["qk_sb"], h + (e + 1))
                            half = C_QK // 2
                            scores(acc[:, 6, 0:KEYS], [q_t[0:half, j * SEQ:(j + 1) * SEQ] for j in range(2)],
                                   [k_t[0:half, j * SEQ:(j + 1) * SEQ] for j in range(2)], C["scored"])

                        def c_p_t():
                            pe.wait_ge(C["p_ready"], h + (e + 1))
                            probs_t(4, e_sb[:, 0], C["p_t"])

                        def c_out():
                            pe.wait_ge(C["p_sb"], h + (e + 1))
                            pe.wait_ge(C["o_out"], h + (e + 1))
                            out_t(7, v_rows, p_t[:, 0], C["o_done"])

                        def b_t():
                            pe.wait_ge(B["staged"], hb + 1)
                            for t in range(NT):
                                mm = pe.transpose(acc[:, 5, t * P:(t + 1) * P], bq_rows[:, t], ident[:, :])
                            mm.then_inc(B["qk_t"], 1)

                        def b_scores():
                            pe.wait_ge(B["qk_sb"], hb + 1)
                            scores(acc[:, 5, 0:KEYS], [bq_t[:, :]], [bk_t[:, :]], B["scored"])

                        def b_p_t():
                            probs_t(5, e_sb[:, 1], B["p_t"])

                        def b_out():
                            pe.wait_ge(B["p_sb"], hb + 1)
                            out_t(5, proj[:, :, BV:BV + P], p_t[:, 1], B["o_done"])

                        after = {2: c_t, 3: c_scores, 6: c_p_t, 7: c_out}
                        after.update({4: b_t, 5: b_scores} if e == 0 else {4: b_p_t, 5: b_out})
                        if e == 0:
                            pe.wait_ge(B["o_out"], hb + 1)
                        whole(n, e * UB, opa, e, after)

                def branches(n, j, after):
                    for r, (pair, k0, us) in enumerate(((0, 4, (0, 1)), (1, 0, (2, 3)), (3, 8, (4, 5, 6, 7)))):
                        pe.wait_ge(dve_emptied, l * DVE_GROUPS + j * 3 + (r + 1))
                        if after is first_chunk:
                            if r == 0:
                                pe.wait_ge(act_emptied, l * ACT_GROUPS + (ACT_GROUPS - 1 + 2))
                                pe.wait_ge(B["o_out"], (l + 1) * B_HEADS + 1)
                            if r == 1:
                                pe.wait_ge(act_emptied, (l + 1) * ACT_GROUPS + 2)
                                pe.wait_ge(ao_lo, l + 1)
                            if r == 2:
                                pe.wait_ge(C["o_out"], (l + 1) * C_HEADS + 1)
                        for u in us:
                            unit(n, u, opb, k0 + KU * (u - us[0]), pair, u == us[0], u == us[-1])
                            if u in after:
                                after[u]()

                def ao_cols():
                    pe.wait_ge(ao_rows, l + 1)
                    rows_to_cols(4, proj[:, :, 0:A_HEADS * A_V]).then_inc(ao_t, 1)

                first_chunk = {0: ao_cols}
                branches(units(l, B_BR), 0, first_chunk)
                with pe.Fori(1, NC) as j:
                    n = pe.snap(units(l, B_BR) + j * UB)

                    def merged_rolled():
                        pe.wait_ge(m_rows, l * NC + j)
                        pe.wait_ge(m_lo, l * NC + j)
                        rows_to_cols(4, nat).then_inc(m_t, 1)

                    branches(n, j, {1: merged_rolled})

                def x_cols(j):
                    pe.wait_ge(dve_emptied, l * DVE_GROUPS + (CREDIT + V_OUT + j + 1))
                    pe.wait_ge(x_lo, l * (2 * NC) + (NC + j))
                    rows_to_cols(4, xs[:, :, j * N:(j + 1) * N]).then_inc(x_t, 1)

                for j in range(NC):
                    pe.wait_ge(dve_emptied, l * DVE_GROUPS + (CREDIT + (V_OUT - 3 + j if j < 2 else V_OUT + j - 2) + 1))

                    def last_merged():
                        pe.wait_ge(m_rows, l * NC + NC)
                        pe.wait_ge(m_lo, l * NC + NC)
                        rows_to_cols(4, nat).then_inc(m_t, 1)

                    def need_m(m):
                        if j == 0 and m == 6:
                            pe.wait_ge(m_lo, l * NC + NC + 1)
                        if j == 0 and m == 0:
                            pe.wait_ge(m_lo, l * NC + NC)

                    def next_x():
                        if j == 1:
                            pe.wait_ge(m_lo, l * NC + NC + 1)
                        x_cols(j - 1)

                    whole(units(l, B_OUT + j), 0, opa, j % 2, {1: last_merged} if j == 0 else {1: next_x}, N, need_m)

                def hidden_t(j):
                    pe.wait_ge(dve_emptied, l * DVE_GROUPS + (j * 2 + (CREDIT + V_FF + 2)))
                    pe.wait_ge(h_sb, l * NF + j + 1)
                    rows_to_cols(4, nat).then_inc(h_t, 1)

                def need_ff(m):
                    if m == 0:
                        pe.wait_ge(x_lo, l * (2 * NC) + (2 * NC - 1))
                    if m == 6:
                        pe.wait_ge(x_lo, l * (2 * NC) + 2 * NC)

                for e in range(2):
                    pe.wait_ge(dve_emptied, l * DVE_GROUPS + (CREDIT + V_FF + e - 1))
                    whole(units(l, B_FF), e * UB, opb, e, {1: lambda: x_cols(NC - 1)} if e == 0 else {}, N,
                          need_ff if e == 0 else None)
                with pe.Fori(1, NF) as j:
                    n = pe.snap(units(l, B_FF) + j * (2 * UB))
                    for e in range(2):
                        pe.wait_ge(dve_emptied, l * DVE_GROUPS + j * 2 + (CREDIT + V_FF + e - 1))
                        if e == 0:
                            whole(n, 0, opb, 0, {1: lambda: hidden_t(j - 1)})
                        else:
                            whole(n, UB, opb, 1, {})

                def down(n, m0, kk, value, first, last, after={}):
                    pe.wait_ge(jit_lo, value)
                    for c in range(NC):
                        if first and c < 2:
                            pe.wait_ge(dve_emptied, l * DVE_GROUPS + (CREDIT + V_DN + c - 1))
                        if first and c == 2:
                            pe.wait_ge(h_sb, l * NF + (NF + 1))
                        for u in range(2):
                            unit(n, m0 + 2 * c + u, opa, 4 * (kk % 2) + KU * u, c, first and u == 0, last and u == 1)
                            if 2 * c + u in after:
                                after[2 * c + u]()

                down(units(l, B_DN), 0, 0, l * NF + 1, True, False, {1: lambda: hidden_t(NF - 1)})
                with pe.Fori(0, (NF - 3) // 2) as i:
                    n = pe.snap(units(l, B_DN + 1) + i * (2 * UB))
                    for e in range(2):
                        down(n, e * UB, 1 + e, l * NF + i * 2 + (e + 2), False, False)
                for e in range(2):
                    down(units(l, BLOCKS - 2 + e), 0, 1 + e, l * NF + (NF - 1 + e), False, e == 1)

        @block.scalar
        def _(act):
            def copy(out, in_, scale=1.0):
                return act.activation(out, in_, ACT.Copy, scale=scale)

            def hi(n, nq, m):
                s = m % RING
                act.wait_ge(raw_landed[s], nq + 16 * (m // RING + 1))
                act.wait_ge(unit_done, n + (m + 1))
                copy(w_hi[:, s], raw[:, s]).then_inc(hi_ready, 1)

            def through(n, nq, m0, after, units_=UB):
                for m in range(UB):
                    if m < units_:
                        hi(n, nq, m0 + m + RING)
                    if m in after:
                        after[m](n)

            def bases(l, blk, i=None, per=1):
                n, q = units(l, blk), l * (BLOCKS * UB * 4) + blk * UB * 4
                if i is None:
                    return n, q
                return act.snap(n + i * (per * UB)), act.snap(q + i * (per * UB * 4))

            def done(n, m):
                act.wait_ge(unit_done, n + (RING + m + 1))

            def root(value, v, r):
                act.wait_ge(var_ready, value)
                act.activation(r, v, ACT.Sqrt).then_inc(root_ready, 1)

            def split_hi(value, t_sem, dst, b0, gain, h_sem):
                act.wait_ge(t_sem, value)
                src = acc[:, b0:b0 + 2, :].rearrange("p b (k s) -> p (b k) s", s=SEQ)
                if gain is None:
                    copy(dst, src).then_inc(h_sem, 1)
                    return
                for k in range(4):
                    ins = copy(dst[:, k], src[:, k], gain[:, k:k + 1])
                ins.then_inc(h_sem, 1)

            def load_gains(l):
                at = 0
                for name, width in GAINS:
                    act.dma_start(gains[:, at:at + width],
                                  gain_of[name][ds(l, 1), :].to_broadcast([P, width])).then_inc(gains_landed, 16)
                    at += width
                act.dma_start(lamb, a_lambda.rearrange("l f d -> l (f d)")[ds(l, 1), :].to_broadcast([P, 4 * A_QK])
                              .rearrange("p (f d) -> p f d", f=4)).then_inc(gains_landed, 16)

            act.dma_start(rope_sb[:, :, :], rope_tab.rearrange("(t p) n -> p t n", p=P)).then_inc(rope_landed, 16)
            act.sem_inc(act_emptied, 2)
            act.wait_ge(pool_const, 6)
            act.sem_inc(m_lo, 1)
            act.sem_inc(h_sb, 1)

            with act.Fori(0, DEPTH) as l:
                n, nq = bases(l, 0)
                hi(n, nq, 0)
                hi(n, nq, 1)
                act.wait_ge(gnow_ready, l + 1)
                for j in range(NC):
                    split_hi(l * (2 * NC) + (j + 1), x_t, opa[0][:, 4 * j:4 * j + 4], 2 * j,
                             gnow[:, 4 * j:4 * j + 4], x_hi)
                    if j < RING - 2:
                        hi(n, nq, j + 2)
                act.wait_ge(gains_free, l + 1)
                load_gains(l)

                def leave_proj(n, m, pair, col):
                    done(n, m)
                    act.wait_ge(rx_ready, l * 2 + 1)
                    for t in range(NT):
                        ins = copy(proj[:, t, ds(col, PC)], bank(pair, t, PC), rx[:, t:t + 1])
                    ins.then_inc(act_emptied, 1)

                through(n, nq, 0, {5: lambda n: root(l * 4 + 1, stats[:, 0:2], root_sb[:, 0:2]),
                                   7: lambda n: leave_proj(n, 7, 0, 0)})
                through(n, nq, UB, {7: lambda n: leave_proj(n, UB + 7, 1, PC)})
                with act.Fori(1, PROJ1 // 2) as i:
                    n, nq = bases(l, 0, i, 2)
                    for e in range(2):
                        through(n, nq, e * UB, {7: lambda n: leave_proj(n, e * UB + 7, e, i * (2 * PC) + e * PC)})

                root(l * 4 + 2, stats[:, 0:44], root_sb[:, 0:44])
                with act.Fori(0, PROJ2 // 2) as i:
                    n, nq = bases(l, PROJ1, i, 2)
                    h = act.snap(l * PROJ2 + i * 2)
                    for e in range(2):
                        def pair_sb(n):
                            act.wait_ge(i_t, h + (e + 1))
                            copy(q_t, acc[:, 4, :])
                            copy(bk_t[:, :], acc[:, 5, 0:SEQ]).then_inc(i_sb, 1)

                        def pair_relu(n):
                            act.wait_ge(i_scored, h + (e + 1))
                            act.wait_ge(i_summed, h + (e + 1))
                            act.activation(s_sb, acc[:, 6:8, 0:KEYS], ACT.Relu).then_inc(i_relu, 1)

                        def leave(n):
                            leave_proj(n, e * UB + 7, e, (PROJ1 + PROJ2 - 1) * PC - e * PC - i * (2 * PC))

                        through(n, nq, e * UB, {4: pair_sb, 6: pair_relu, 7: leave})

                split_hi(l + 1, ckv_t, opb[0][:, 0:4], 4, gnow[:, 2 * KT:2 * KT + 4], ckv_hi)

                act.wait_ge(lam_dots, l + 1)
                act.activation(lam[:, 2:4], lam[:, 0:2], ACT.Exp).then_inc(lam_exp, 1)

                def save_gate(n, m, e, value, chunk, saved):
                    done(n, m)
                    act.wait_ge(gate_saved, saved)
                    for t in range(NT):
                        ins = copy(nat[:, t], bank(e, t), rx[:, t:t + 1])
                    ins.then_inc(act_emptied, 1)
                    act.wait_ge(act_emptied, value)
                    act.dma_start(gate_store[ds(chunk, 1)].rearrange("a p n -> p (a n)"),
                                  nat.rearrange("p t n -> p (t n)")).then_inc(gate_saved, 16)

                def exps(S, value, maps):
                    act.wait_ge(S["maxed"], value)
                    for m in maps:
                        for t, (a, b) in enumerate(SEG):
                            ins = act.activation(e_sb[:, m, a:b], s_sb[:, m, a:b], ACT.Exp, bias=nmax[:, m, t:t + 1],
                                                 accum_out=sums[:, m, t:t + 1])
                    ins.then_inc(S["exped"], 1)

                A, B, C = head["a"], head["b"], head["c"]
                with act.Fori(0, A_HEADS // 2) as i:
                    n, nq = bases(l, B_A, i, 2)
                    h = act.snap(l * A_HEADS + i * 2)
                    for e in range(2):
                        def a_qk_sb(n):
                            act.wait_ge(A["qk_t"], h + (e + 1))
                            copy(q_t, acc[:, 4, :]).then_inc(A["qk_sb"], 1)

                        def a_p_sb(n):
                            act.wait_ge(A["p_t"], h + (e + 1))
                            copy(p_t[:, 0], acc[:, 4, 0:KEYS]).then_inc(A["p_sb"], 1)

                        def a_o(n):
                            act.wait_ge(A["o_done"], h + (e + 1))
                            copy(proj[:, :, ds(AQ + i * (2 * A_V) + e * A_V, A_V)],
                                 acc[:, 7, 0:SEQ].rearrange("p (t n) -> p t n", t=NT)).then_inc(A["o_out"], 1)

                        def leave(n):
                            save_gate(n, e * UB + 7, e, l * ACT_GROUPS + i * 2 + (2 + G_A + e + 1),
                                      l * NG + i * 2 + e, l * (NG * 16) + i * 32 + (16 * e + 16))

                        def a_o_leave(n):
                            a_o(n)
                            leave(n)

                        through(n, nq, e * UB, {1: a_qk_sb, 3: lambda n: exps(A, h + (e + 1), (0, 1)),
                                                5: a_p_sb, 7: a_o_leave})

                n, nq = bases(l, B_KV)

                def leave_kv(m):
                    j = m // 2
                    done(n, m)
                    copy(kv_rows[:, :, j * N:(j + 1) * N], bank(j % 2)).then_inc(act_emptied, 1)

                through(n, nq, 0, {m: (lambda n, m=m: leave_kv(m)) for m in (1, 3, 5, 7)})
                root(l * 4 + 3, stats[:, 0:42], root_sb[:, 0:42])

                with act.Fori(0, C_HEADS // 2) as i:
                    n, nq = bases(l, B_C, i, 2)
                    h = act.snap(l * C_HEADS + i * 2)
                    hb = act.snap(l * B_HEADS + i)
                    for e in range(2):
                        def c_qk_sb(n):
                            act.wait_ge(C["qk_t"], h + (e + 1))
                            half = C_QK // 2
                            copy(q_t[0:half, :], acc[0:half, 4, :])
                            copy(k_t[0:half, :], acc[0:half, 5, :]).then_inc(C["qk_sb"], 1)

                        def c_exps(n):
                            exps(C, h + (e + 1), (0,))

                        def b_sb(n):
                            if e == 0:
                                act.wait_ge(B["qk_t"], hb + 1)
                                copy(bq_t[:, :], acc[:, 5, 0:SEQ]).then_inc(B["qk_sb"], 1)
                            else:
                                act.wait_ge(B["p_t"], hb + 1)
                                copy(p_t[:, 1], acc[:, 5, 0:KEYS]).then_inc(B["p_sb"], 1)

                        def c_p_sb(n):
                            act.wait_ge(C["p_t"], h + (e + 1))
                            copy(p_t[:, 0], acc[:, 4, 0:KEYS]).then_inc(C["p_sb"], 1)

                        def b_exps(n):
                            exps(B, hb + 1, (1,))

                        def b_o(n):
                            act.wait_ge(B["o_done"], hb + 1)
                            copy(opb[0][:, ds(i + A_HEADS, 1), :].rearrange("p a s -> p (a s)"),
                                 acc[:, 5, 0:SEQ]).then_inc(B["o_hi"], 1)

                        def c_o(n):
                            act.wait_ge(C["o_done"], h + (e + 1))
                            copy(opb[0][:, ds(i * 2 + (A_HEADS + B_HEADS + e), 1), :].rearrange("p a s -> p (a s)"),
                                 acc[:, 7, 0:SEQ]).then_inc(C["o_hi"], 1)

                        def leave(n):
                            save_gate(n, e * UB + 7, e, l * ACT_GROUPS + i * 2 + (2 + G_C + e + 1),
                                      l * NG + i * 2 + (A_HEADS + e), l * (NG * 16) + i * 32 + (16 * (A_HEADS + e) + 16))

                        def exps_sb(n):
                            c_exps(n)
                            b_sb(n)

                        def p_b(n):
                            c_p_sb(n)
                            if e == 0:
                                b_exps(n)

                        def leave_o(n):
                            leave(n)
                            c_o(n)

                        after = {2: c_qk_sb, 4: exps_sb, 6: p_b, 7: leave_o}
                        if e == 1:
                            after[5] = b_o
                        through(n, nq, e * UB, after)

                def load_gate(r, piece, j):
                    act.dma_start(gates[:, ds(piece, 1)].rearrange("p k n -> p (k n)"),
                                  gate_store[ds(l * NG + BRANCH_ORDER[r] * NC + j, 1)].rearrange("a p n -> p (a n)"))\
                        .then_inc(gate_back[r], 16)

                def open_piece(r):
                    act.wait_ge(gate_back[r], l * (NC * 16) + 16)
                    g = gates[:, FIRST_PIECES[r]]
                    act.activation(g, g, ACT.Sigmoid).then_inc(gate_open, 1)

                def open_chunk(j):
                    for r in range(3):
                        act.wait_ge(gate_back[r], l * (NC * 16) + j * 16 + 16)
                    g = gates[:, ds(4 * j - 2, 3)].rearrange("p k n -> p (k n)")
                    act.activation(g, g, ACT.Sigmoid).then_inc(gate_open, 3)

                def merged_hi(value, j):
                    split_hi(value, m_t, opa[0][:, ds(j * 4, 4)], 4, None, m_hi)

                def ao_first(n):
                    split_hi(l + 1, ao_t, opb[0][:, 0:4], 4, None, ao_hi)
                    act.wait_ge(C["o_out"], (l + 1) * C_HEADS + 1)
                    load_gate(2, FIRST_PIECES[2], 0)

                def all_saved(n):
                    act.wait_ge(gate_saved, (l + 1) * (NG * 16) + 16)
                    open_piece(0)

                def open_and_load_1(n):
                    open_piece(1)
                    load_gate(0, 2, 1)

                def open_and_load_2(n):
                    open_piece(2)
                    load_gate(1, 3, 1)

                load_gate(0, FIRST_PIECES[0], 0)
                load_gate(1, FIRST_PIECES[1], 0)
                n, nq = bases(l, B_BR)
                through(n, nq, 0, {0: ao_first, 1: all_saved, 2: open_and_load_1, 4: open_and_load_2,
                                   6: lambda n: load_gate(2, 4, 1)})
                with act.Fori(1, NC - 1) as j:
                    n, nq = bases(l, B_BR, j)

                    def open_and_load(n):
                        open_chunk(j)
                        load_gate(0, 4 * j + 2, j + 1)

                    through(n, nq, 0, {1: lambda n: merged_hi(l * NC + j, j - 1), 2: open_and_load,
                                       4: lambda n: load_gate(1, 4 * j + 3, j + 1),
                                       6: lambda n: load_gate(2, 4 * j + 4, j + 1)})
                n, nq = bases(l, B_OUT - 1)
                through(n, nq, 0, {1: lambda n: merged_hi(l * NC + NC - 1, NC - 2), 3: lambda n: open_chunk(NC - 1)})

                def x_hi_of(j):
                    split_hi(l * (2 * NC) + (NC + j + 1), x_t, opb[0][:, 4 * j:4 * j + 4], 4,
                             gnow[:, KT + 4 * j:KT + 4 * j + 4], x_hi)

                for j in range(NC):
                    n, nq = bases(l, B_OUT + j)
                    through(n, nq, 0, {1: (lambda n: merged_hi(l * NC + NC, NC - 1)) if j == 0 else
                                       (lambda n: x_hi_of(j - 1))})

                def sigmoids(n, m, value):
                    done(n, m)
                    act.wait_ge(dve_emptied, value)
                    for t in range(NT):
                        ins = act.activation(sg[:, t], bank(0, t), ACT.Sigmoid, scale=rx[:, 2 + t:3 + t])
                    ins.then_inc(sig_ready, 1)

                def hidden_sb(value, j):
                    act.wait_ge(h_t, value)
                    copy(hid_t[:, ds(j * 4, 4)], acc[:, 4:6, :].rearrange("p b (k s) -> p (b k) s", s=SEQ))\
                        .then_inc(h_sb, 1)

                n, nq = bases(l, B_FF)

                def first_ffn(n):
                    root(l * 4 + 4, stats[:, 0:2], root_sb[:, 0:2])

                def first_sig(n):
                    act.wait_ge(rx_ready, l * 2 + 2)
                    sigmoids(n, UB - 1, l * DVE_GROUPS + (CREDIT + V_FF))

                through(n, nq, 0, {1: lambda n: x_hi_of(NC - 1), 4: first_ffn, 7: first_sig})
                through(n, nq, UB, {})
                with act.Fori(1, NF - 1) as j:
                    n, nq = bases(l, B_FF, j, 2)
                    through(n, nq, 0, {1: lambda n: hidden_sb(l * NF + j, j - 1),
                                       7: lambda n: sigmoids(n, UB - 1, l * DVE_GROUPS + j * 2 + (CREDIT + V_FF))})
                    through(n, nq, UB, {})

                def jit(value, kk, slot):
                    act.wait_ge(h_sb, value)
                    copy(opa[0][:, 4 * slot:4 * slot + 4], hid_t[:, ds(kk * 4, 4)]).then_inc(jit_hi, 1)

                n, nq = bases(l, B_FF + 2 * (NF - 1))
                through(n, nq, 0, {1: lambda n: hidden_sb(l * NF + NF - 1, NF - 2), 4: lambda n: jit(l * NF + 2, 0, 0),
                                   7: lambda n: sigmoids(n, UB - 1, l * DVE_GROUPS + (2 * (NF - 1) + CREDIT + V_FF))})
                n, nq = bases(l, B_DN - 1)
                through(n, nq, 0, {4: lambda n: jit(l * NF + 3, 1, 1)})
                n, nq = bases(l, B_DN)
                through(n, nq, 0, {1: lambda n: hidden_sb(l * NF + NF, NF - 1)})
                with act.Fori(0, (NF - 3) // 2) as i:
                    n, nq = bases(l, B_DN + 1, i, 2)
                    for e in range(2):
                        through(n, nq, e * UB, {1: lambda n: jit(l * NF + i * 2 + (e + 4), i * 2 + (e + 2), e)})
                n, nq = bases(l, BLOCKS - 2)
                through(n, nq, 0, {1: lambda n: jit(l * NF + (NF + 1), NF - 1, 0)})
                n, nq = bases(l, BLOCKS - 1)
                through(n, nq, 0, {}, UB - RING)

        @block.vector
        def _(dve):
            step = Steps(dve, dve_step, dve_mark)

            def wait(s, v):
                dve.wait_ge(s, v)

            def tt(out, a, b, op):
                return dve.tensor_tensor(out, a, b, op)

            def bc(ap, n):
                return ap.unsqueeze(3).to_broadcast([P, ap.shape[1], ap.shape[2], n])

            def over(ap, h):
                return ap.unsqueeze(2).to_broadcast([P, ap.shape[1], h, ap.shape[2]])

            def gain(at, d, h):
                return gains[:, at:at + d].unsqueeze(1).unsqueeze(1).to_broadcast([P, NT, h, d])

            def heads(ap, h):
                return ap.rearrange("p t (h d) -> p t h d", h=h)

            def squares(src, dst):
                h, d = src.shape[2], src.shape[3]
                v = tmp[:, 0:NT * h * d].rearrange("p (t h d) -> p t h d", t=NT, h=h)
                step(tt(v, src, src, ALU.mult))
                step(dve.tensor_reduce(dst, v, AX, ALU.add))

            def rope(X, h, rot, at):
                half = rot // 2
                ta = tmp[:, 0:NT * h * rot].rearrange("p (t h d) -> p t h d", t=NT, h=h)
                tb = tmp[:, 512:512 + NT * h * rot].rearrange("p (t h d) -> p t h d", t=NT, h=h)
                cc, ss = rope_sb[:, :, at:at + rot], rope_sb[:, :, at + rot:at + 2 * rot]
                step(tt(ta, X[:, :, :, 0:rot], over(cc, h), ALU.mult), False)
                step(tt(tb[:, :, :, 0:half], X[:, :, :, half:rot], over(ss[:, :, 0:half], h), ALU.mult), False)
                step(tt(tb[:, :, :, half:rot], X[:, :, :, 0:half], over(ss[:, :, half:rot], h), ALU.mult))
                step(tt(X[:, :, :, 0:rot], ta, tb, ALU.add))

            def mean(a, b, d):
                return dve.tensor_scalar(stats[:, a:b], stats[:, a:b], 1.0 / d, EPS, ALU.mult, ALU.add)

            def reciprocal_roots(value, n, out, ready):
                v, r, y, z = stats[:, 0:n], root_sb[:, 0:n], tmp[:, 0:n], tmp[:, 64:64 + n]
                wait(root_ready, value)
                step(dve.reciprocal(y, r))
                step(tt(z, v, y, ALU.mult))
                step(tt(z, z, y, ALU.mult))
                step(dve.tensor_scalar(z, z, -0.5, 1.5, ALU.mult, ALU.add))
                tt(out, y, z, ALU.mult).then_inc(ready, 1)

            def chunk_squares(j):
                v = tmp[:, 0:NT * N].rearrange("p (t n) -> p t n", t=NT)
                c = xs[:, :, j * N:(j + 1) * N]
                step(tt(v, c, c, ALU.mult))
                step(dve.tensor_reduce(xsq[:, :, j], v, AX, ALU.add))

            def row_factors(l, which, value):
                step(dve.tensor_reduce(stats[:, 0:NT], xsq[:, :, :], AX, ALU.add))
                mean(0, NT, D).then_inc(var_ready, 1)
                wait(var_ready, value)
                reciprocal_roots(value, NT, rx[:, 2 * which:2 * which + 2], rx_ready)
                wait(rx_ready, l * 2 + which + 1)

            def split_lo(value, h_sem, hi_, lo_, b0, gain_, l_sem):
                wait(h_sem, value)
                src = acc[:, b0:b0 + 2, :].rearrange("p b (k s) -> p (b k) s", s=SEQ)
                if gain_ is None:
                    tt(lo_, src, hi_.bitcast(F32), ALU.subtract).then_inc(l_sem, 1)
                    return
                for k in range(4):
                    ins = dve.scalar_tensor_tensor(lo_[:, k], src[:, k], gain_[:, k:k + 1], hi_[:, k].bitcast(F32),
                                                   ALU.mult, ALU.subtract)
                ins.then_inc(l_sem, 1)

            def softmax_in(S, value, b0, maps, scale, mask):
                m0, m1 = maps[0], maps[-1] + 1
                k = m1 - m0
                wait(S["scored"], value)
                step(dve.scalar_tensor_tensor(s_sb[:, m0:m1], acc[:, b0:b0 + k, 0:KEYS], scale,
                                              mask.unsqueeze(1).to_broadcast([P, k, KEYS]), ALU.mult, ALU.add))
                for t, (a, b) in enumerate(SEG):
                    ins = dve.tensor_reduce(nmax[:, m0:m1, t], s_sb[:, m0:m1, a:b], AX, ALU.max, negate=True)
                    if t == 0:
                        step(ins, False)
                ins.then_inc(S["maxed"], 1)

            def softmax_out(S, value, m):
                wait(S["exped"], value)
                step(dve.reciprocal(rsum[:, m], sums[:, m]))
                for t, (a, b) in enumerate(SEG):
                    ins = dve.tensor_scalar(e_sb[:, m, a:b], e_sb[:, m, a:b], rsum[:, m, t:t + 1], None, ALU.mult)
                    if t == 0:
                        step(ins, False)
                ins.then_inc(S["p_ready"], 1)

            for l_ in range(DEPTH):
                init = 0.8 - 0.6 * math.exp(-0.3 * l_)
                step(dve.memset(laminit[:, l_, 0:1], init), False)
                step(dve.memset(laminit[:, l_, 1:2], 1.0 - init))
            dve.sem_inc(dve_emptied, CREDIT)
            dve.sem_inc(gains_free, 1)
            dve.sem_inc(i_summed, 1)
            dve.sem_inc(head["a"]["o_out"], 1)
            dve.sem_inc(head["b"]["o_out"], 1)
            dve.sem_inc(head["c"]["o_out"], 1)
            dve.sem_inc(gate_saved, 16)
            wait(gcol_t, 1)
            step(dve.tensor_copy(gcol[:, :], acc[:, 7, 0:72]))
            wait(pool_const, 6)
            for j in range(NC):
                wait(x_landed[j], 16)
                dve.sem_inc(x_now, 1)

            LAYER = 1500
            step.hold()
            with dve.Fori(0, DEPTH) as l, step.turn(l, DEPTH, LAYER):
                A, B, C = head["a"], head["b"], head["c"]
                step(dve.tensor_copy(gnow[:, 0:KT], gcol[:, ds(l * KT, KT)]), False)
                step(dve.tensor_copy(gnow[:, KT:2 * KT], gcol[:, ds(l * KT + DEPTH * KT, KT)]), False)
                step(dve.tensor_copy(gnow[:, 2 * KT:], gcol[:, ds(l * 4 + 2 * DEPTH * KT, 4)]))
                dve.sem_inc(gnow_ready, 1)
                row_stats = l * 4 + 1
                for j in range(NC):
                    split_lo(l * (2 * NC) + (j + 1), x_hi, opa[0][:, 4 * j:4 * j + 4], opa[1][:, 4 * j:4 * j + 4],
                             2 * j, gnow[:, 4 * j:4 * j + 4], x_lo)
                for j in range(NC):
                    chunk_squares(j)
                row_factors(l, 0, row_stats)

                wait(gains_landed, (l + 1) * (16 * (len(GAINS) + 1)))
                wait(rope_landed, 16)
                dots = tmp[:, 0:2 * A_QK].rearrange("p (f d) -> p f d", f=2)
                step(tt(dots, lamb[:, 0::2], lamb[:, 1::2], ALU.mult))
                dve.tensor_reduce(lam[:, 0:2], dots, AX, ALU.add).then_inc(lam_dots, 1)
                step(dve.tensor_scalar(gains[:, GSUB:GSUB + A_V], gains[:, GSUB:GSUB + A_V],
                                       laminit[:, ds(l, 1), 1:2].rearrange("p a b -> p (a b)"), None, ALU.mult))

                def projected(block):
                    wait(act_emptied, l * ACT_GROUPS + (2 + block + 1))

                s_a = stats[:, 0:32].rearrange("p (t h) -> p t h", t=NT)
                projected(AK // PC)
                squares(heads(proj[:, :, AQ:AK], 8), s_a[:, :, 0:8])
                projected(AV // PC)
                squares(heads(proj[:, :, AK:AV], 8), s_a[:, :, 8:16])
                projected(BK // PC)
                squares(heads(proj[:, :, BQ:BK], 4), stats[:, 34:42].rearrange("p (t h) -> p t h", t=NT))
                squares(heads(proj[:, :, BK:BV], 1), stats[:, 42:44].rearrange("p (t h) -> p t h", t=NT))
                projected(PROJ1 - 1)
                squares(heads(proj[:, :, IK:IW], 1), stats[:, 32:34].rearrange("p (t h) -> p t h", t=NT))
                step(mean(0, 34, A_QK))
                mean(34, 44, B_DIM).then_inc(var_ready, 1)
                wait(var_ready, l * 4 + 2)
                reciprocal_roots(l * 4 + 2, 44, rs[:, 0:44], rs_ready)
                wait(rs_ready, l * 2 + 1)
                r_a = rs[:, 0:32].rearrange("p (t h) -> p t h", t=NT)
                r_ik = rs[:, 32:34].rearrange("p (t h) -> p t h", t=NT)
                r_bq = rs[:, 34:42].rearrange("p (t h) -> p t h", t=NT)
                r_bk = rs[:, 42:44].rearrange("p (t h) -> p t h", t=NT)

                def normed(X, h, d, r, g, rot, at):
                    step(tt(X, X, bc(r, d), ALU.mult))
                    step(tt(X, X, g, ALU.mult))
                    rope(X, h, rot, at)

                normed(heads(proj[:, :, IK:IW], 1), 1, I_DIM, r_ik, gain(GIK, I_DIM, 1), ROT["a"], ROPE_AT["a"])
                for m in range(2):
                    step(dve.tensor_copy(ik_rows[:, :, m * I_DIM:(m + 1) * I_DIM], proj[:, :, IK:IW]), False)
                rope(heads(proj[:, :, IQ:IK], I_HEADS), I_HEADS, ROT["a"], ROPE_AT["a"])
                step(dve.tensor_scalar(iws[:, :, :], proj[:, :, IW:IW + I_HEADS], I_HEADS ** -0.5 * I_DIM ** -0.5, None,
                                       ALU.mult), False)
                normed(heads(proj[:, :, BK:BV], 1), 1, B_DIM, r_bk, gain(GBK, B_DIM, 1), ROT["b"], ROPE_AT["b"])
                step(dve.memset(score_i[:, :], 0.0))

                step.hold()
                with dve.Fori(0, PROJ2) as i, step.turn(i, PROJ2, 64):
                    dve.tensor_copy(bq_rows, proj[:, :, ds(IQ + i * P, P)]).then_inc(i_staged, 1)
                    a4 = heads(proj[:, :, ds(AQ + i * (4 * A_QK), 4 * A_QK)], 4)
                    g4 = gains[:, ds(GA + i * A_QK, A_QK)].unsqueeze(1).unsqueeze(1).to_broadcast([P, NT, 4, A_QK])
                    normed(a4, 4, A_QK, r_a[:, :, ds(i * 4, 4)], g4, ROT["a"], ROPE_AT["a"])
                    b1 = heads(proj[:, :, ds(BQ + i * B_DIM, B_DIM)], 1)
                    normed(b1, 1, B_DIM, r_bq[:, :, ds(i, 1)], gain(GBQ, B_DIM, 1), ROT["b"], ROPE_AT["b"])
                    wait(i_relu, l * PROJ2 + i + 1)
                    for m in range(2):
                        for t, (a, b) in enumerate(SEG):
                            ins = dve.scalar_tensor_tensor(score_i[:, a:b], s_sb[:, m, a:b],
                                                           iws[:, t, ds(i * 2 + m, 1)], score_i[:, a:b],
                                                           ALU.mult, ALU.add)
                            if (m, t) != (1, 1):
                                step(ins, (m, t) == (0, 1))
                    ins.then_inc(i_summed, 1)
                    wait(i_summed, l * PROJ2 + i + 2)

                split_lo(l + 1, ckv_hi, opb[0][:, 0:4], opb[1][:, 0:4], 4, gnow[:, 2 * KT:2 * KT + 4], ckv_lo)
                step(tt(score_i[:, :], score_i[:, :], causal[:, :], ALU.add))
                wait(lam_exp, l + 1)
                step(tt(lam[:, 4:5], lam[:, 2:3], lam[:, 3:4], ALU.subtract))
                step(dve.tensor_scalar(lam[:, 5:6], lam[:, 4:5], laminit[:, ds(l, 1), 0:1].rearrange("p a b -> p (a b)"),
                                       None, ALU.add))

                r_cq = stats[:, 0:16].rearrange("p (t h) -> p t h", t=NT)
                step.hold()
                with dve.Fori(0, A_HEADS) as i, step.turn(i, A_HEADS, 64):
                    h = l * A_HEADS + i
                    wait(A["o_out"], h + 1)
                    for m, at in enumerate((AQ, AK)):
                        step(dve.tensor_copy(qk_rows[:, m], proj[:, :, ds(at + i * P, P)]), False)
                    dve.tensor_copy(v_rows, proj[:, :, ds(AV + i * P, P)]).then_inc(A["staged"], 1)
                    squares(heads(proj[:, :, ds(CQ + i * (2 * C_QK), 2 * C_QK)], 2), r_cq[:, :, ds(i * 2, 2)])
                    softmax_in(A, h + 1, 5, (0, 1), A_QK ** -0.5, causal[:, :])
                    wait(A["exped"], h + 1)
                    step(dve.reciprocal(rsum[:, :, :], sums[:, :, :]))
                    step(dve.tensor_scalar(rsum[:, 1], rsum[:, 1], lam[:, 5:6], None, ALU.mult))
                    for t, (a, b) in enumerate(SEG):
                        step(dve.tensor_scalar(e_sb[:, 1, a:b], e_sb[:, 1, a:b], rsum[:, 1, t:t + 1], None, ALU.mult), t == 1)
                    for t, (a, b) in enumerate(SEG):
                        ins = dve.scalar_tensor_tensor(e_sb[:, 0, a:b], e_sb[:, 0, a:b], rsum[:, 0, t:t + 1],
                                                       e_sb[:, 1, a:b], ALU.mult, ALU.subtract)
                        if t == 0:
                            step(ins, False)
                    ins.then_inc(A["p_ready"], 1)
                    for _ in range(TOPK // 8 // A_HEADS):
                        step.hold()
                        for t, (a, b) in enumerate(SEG):
                            step(dve.max(top8[:, t], score_i[:, a:b]), t == 1)
                        step.hold()
                        for t, (a, b) in enumerate(SEG):
                            step(dve.match_replace(score_i[:, a:b], top8[:, t], score_i[:, a:b], TAKEN), t == 1)

                step(dve.tensor_scalar(score_i[:, :], score_i[:, :], TAKEN, NEG, ALU.not_equal, ALU.mult))
                step(tt(score_i[:, :], score_i[:, :], causal[:, :], ALU.min))

                wait(A["o_out"], (l + 1) * A_HEADS + 1)
                s_ck = stats[:, 16:32].rearrange("p (t h) -> p t h", t=NT)
                squares(heads(proj[:, :, 0:A_HEADS * A_V], A_HEADS), stats[:, 32:40].rearrange("p (t h) -> p t h", t=NT))
                squares(heads(proj[:, :, CKV:CKR], 1), stats[:, 40:42].rearrange("p (t h) -> p t h", t=NT))
                squares(heads(proj[:, :, CKR:GATES], 1), stats[:, 42:44].rearrange("p (t h) -> p t h", t=NT))
                step(mean(0, 16, C_QK), False)
                step(mean(32, 40, A_V), False)
                step(mean(40, 42, C_RANK))
                step(dve.reciprocal(stats[:, 44:46], stats[:, 40:42]))
                kr = krot[:, :, :].unsqueeze(2)
                step(tt(kr, heads(proj[:, :, CKR:GATES], 1), gain(GCK, C_ROPE, 1), ALU.mult))
                rope(kr, 1, C_ROPE, ROPE_AT["c"])
                for j in range(NC):
                    wait(act_emptied, l * ACT_GROUPS + (2 + G_KV + j + 1))
                    squares(kv[:, :, 2 * j:2 * j + 2, 0:C_NOPE], s_ck[:, :, 2 * j:2 * j + 2])
                step(tt(s_ck, s_ck, stats[:, 44:46].unsqueeze(2).to_broadcast([P, NT, C_HEADS]), ALU.mult))
                step(tt(s_ck, s_ck, stats[:, 42:44].unsqueeze(2).to_broadcast([P, NT, C_HEADS]), ALU.add))
                mean(16, 32, C_QK).then_inc(var_ready, 1)
                wait(var_ready, l * 4 + 3)
                reciprocal_roots(l * 4 + 3, 42, rs[:, 48:90], rs_ready)
                wait(rs_ready, l * 2 + 2)
                r_cq2 = rs[:, 48:64].rearrange("p (t h) -> p t h", t=NT)
                r_ck = rs[:, 64:80].rearrange("p (t h) -> p t h", t=NT)
                r_ao = rs[:, 80:88].rearrange("p (t h) -> p t h", t=NT)
                r_kv = rs[:, 88:90]
                step(tt(rck[:, :, :], r_ck, r_kv.unsqueeze(2).to_broadcast([P, NT, C_HEADS]), ALU.mult))

                step.hold()
                with dve.Fori(0, C_HEADS // 2) as i, step.turn(i, C_HEADS // 2, 64):
                    h = l * C_HEADS + i * 2
                    hb = l * B_HEADS + i

                    def stage_c(e):
                        j = i * 2 + e
                        wait(C["o_out"], h + (e + 1))
                        q4, k4 = q_rows.unsqueeze(2), k_rows.unsqueeze(2)
                        step(tt(q4, heads(proj[:, :, ds(CQ + i * (2 * C_QK) + e * C_QK, C_QK)], 1),
                                bc(r_cq2[:, :, ds(j, 1)], C_QK), ALU.mult))
                        step(tt(k4[:, :, :, 0:C_ROPE], krot[:, :, :].unsqueeze(2), bc(r_ck[:, :, ds(j, 1)], C_ROPE), ALU.mult), False)
                        step(tt(k4[:, :, :, C_ROPE:], kv[:, :, ds(j, 1), 0:C_NOPE], bc(rck[:, :, ds(j, 1)], C_NOPE), ALU.mult), False)
                        step(tt(v_rows.unsqueeze(2), kv[:, :, ds(j, 1), C_NOPE:], bc(r_kv.unsqueeze(2), C_V), ALU.mult), False)
                        step(tt(q4, q4, gain(GCQ, C_QK, 1), ALU.mult))
                        rope(q4, 1, C_ROPE, ROPE_AT["c"])
                        tt(k4[:, :, :, C_ROPE:], k4[:, :, :, C_ROPE:], gain(GCK + C_ROPE, C_NOPE, 1), ALU.mult)\
                            .then_inc(C["staged"], 1)

                    def out_lo(S, value, b, kt):
                        wait(S["o_hi"], value)
                        at = ds(kt, 1)
                        tt(opb[1][:, at, :], acc[:, b:b + 1, 0:SEQ], opb[0][:, at, :].bitcast(F32), ALU.subtract)\
                            .then_inc(S["o_out"], 1)

                    stage_c(0)
                    dve.tensor_copy(bq_rows, proj[:, :, ds(BQ + i * B_DIM, B_DIM)]).then_inc(B["staged"], 1)
                    softmax_in(C, h + 1, 6, (0,), C_QK ** -0.5, causal[:, :])
                    softmax_out(C, h + 1, 0)
                    softmax_in(B, hb + 1, 5, (1,), B_DIM ** -0.5, score_i[:, :])
                    softmax_out(B, hb + 1, 1)
                    out_lo(C, h + 1, 7, i * 2 + (A_HEADS + B_HEADS))
                    stage_c(1)
                    softmax_in(C, h + 2, 6, (0,), C_QK ** -0.5, causal[:, :])
                    softmax_out(C, h + 2, 0)
                    out_lo(B, hb + 1, 5, i + A_HEADS)
                    out_lo(C, h + 2, 7, i * 2 + (A_HEADS + B_HEADS + 1))

                ao = heads(proj[:, :, 0:A_HEADS * A_V], A_HEADS)
                step(tt(ao, ao, bc(r_ao, A_V), ALU.mult))
                step(tt(ao, ao, gain(GSUB, A_V, A_HEADS), ALU.mult))
                dve.sem_inc(gains_free, 1)
                dve.sem_inc(ao_rows, 1)
                split_lo(l + 1, ao_hi, opb[0][:, 0:4], opb[1][:, 0:4], 4, None, ao_lo)

                m_ = nat[:, :, :]

                def merge_part(j, n, e0, r, piece):
                    pair, last = ((0, 1), (1, 3), (3, 7))[r]
                    wait(unit_done, n + (RING + last + 1))
                    wait(gate_open, l * (NC * 3) + j * 3 + (r + 1))
                    gate = gates[:, ds(piece, 1)].rearrange("p k (t n) -> p (k t) n", t=NT)
                    tt(t_row if r else m_, bank(pair), gate, ALU.mult).then_inc(dve_emptied, 1)
                    wait(dve_emptied, e0 + (CREDIT + r + 1))
                    if r == 1:
                        step(tt(m_, m_, t_row, ALU.add))
                    if r == 2:
                        tt(m_, m_, t_row, ALU.add).then_inc(m_rows, 1)

                def merged_lo(value, j):
                    split_lo(value, m_hi, opa[0][:, ds(j * 4, 4)], opa[1][:, ds(j * 4, 4)], 4, None, m_lo)

                for r in range(3):
                    merge_part(0, units(l, B_BR), l * DVE_GROUPS, r, FIRST_PIECES[r])
                with dve.Fori(1, NC) as j, step.turn(j - 1, NC - 1, 16):
                    n = dve.snap(units(l, B_BR) + j * UB)
                    e0 = dve.snap(l * DVE_GROUPS + j * 3)
                    merged_lo(l * NC + j, j - 1)
                    for r in range(3):
                        merge_part(j, n, e0, r, j * 4 + (r - 2))
                merged_lo(l * NC + NC, NC - 1)

                for j in range(NC):
                    wait(unit_done, units(l, B_OUT + j) + (RING + UB))
                    c = slice(j * N, (j + 1) * N)
                    tt(xs[:, :, c], xs[:, :, c], bank(j % 2), ALU.add).then_inc(dve_emptied, 1)
                    wait(dve_emptied, l * DVE_GROUPS + (CREDIT + V_OUT + j + 1))
                    split_lo(l * (2 * NC) + (NC + j + 1), x_hi, opb[0][:, 4 * j:4 * j + 4], opb[1][:, 4 * j:4 * j + 4],
                             4, gnow[:, KT + 4 * j:KT + 4 * j + 4], x_lo)
                    chunk_squares(j)
                row_factors(l, 1, l * 4 + 4)

                def gate_part(j, e0):
                    wait(sig_ready, l * NF + j + 1)
                    for t in range(NT):
                        ins = dve.scalar_tensor_tensor(gg[:, t], bank(0, t), rx[:, 2 + t:3 + t], sg[:, t],
                                                       ALU.mult, ALU.mult)
                        if t == 0:
                            step(ins, False)
                    ins.then_inc(dve_emptied, 1)
                    wait(dve_emptied, e0 + (CREDIT + V_FF + 1))

                def up_part(j, n):
                    wait(unit_done, n + (RING + 2 * UB))
                    wait(h_sb, l * NF + j + 1)
                    for t in range(NT):
                        ins = dve.scalar_tensor_tensor(nat[:, t], bank(1, t), rx[:, 2 + t:3 + t], gg[:, t],
                                                       ALU.mult, ALU.mult)
                        if t == 0:
                            step(ins, False)
                    ins.then_inc(dve_emptied, 1)

                def jit(value, kk, slot):
                    wait(jit_hi, value)
                    s = slice(4 * slot, 4 * slot + 4)
                    tt(opa[1][:, s], hid_t[:, ds(kk * 4, 4)], opa[0][:, s].bitcast(F32), ALU.subtract).then_inc(jit_lo, 1)

                step.hold()
                with dve.Fori(0, NF - 1) as j, step.turn(j, NF - 1, 16):
                    n = dve.snap(units(l, B_FF) + j * (2 * UB))
                    gate_part(j, dve.snap(l * DVE_GROUPS + j * 2))
                    up_part(j, n)
                jit(l * NF + 1, 0, 0)
                gate_part(NF - 1, l * DVE_GROUPS + 2 * (NF - 1))
                jit(l * NF + 2, 1, 1)
                up_part(NF - 1, units(l, B_FF + 2 * (NF - 1)))

                with dve.Fori(0, (NF - 3) // 2) as i:
                    for e in range(2):
                        jit(l * NF + i * 2 + (e + 3), i * 2 + (e + 2), e)
                jit(l * NF + NF, NF - 1, 0)

                for j in range(NC):
                    wait(unit_done, units(l, BLOCKS - 1) + (RING + 2 * j + 2))
                    c = slice(j * N, (j + 1) * N)
                    tt(xs[:, :, c], xs[:, :, c], bank(j), ALU.add).then_inc(dve_emptied, 1)
                    wait(dve_emptied, l * DVE_GROUPS + (CREDIT + V_DN + j + 1))
                    dve.sem_inc(x_now, 1)


_INS = ['x', 'attn_norm', 'w_in', 'a_q_norm', 'a_k_norm', 'a_lambda', 'a_sub_norm', 'b_q_norm', 'b_k_norm',
        'idx_k_norm', 'c_q_norm', 'c_kv_norm', 'w_kv_b', 'c_k_norm', 'w_branch', 'w_out', 'ffn_norm',
        'w_gate_up', 'w_down']


def kernel(**inputs):
    import numpy as _np
    import concourse.bacc as _bacc
    from concourse import mybir as _mybir
    from concourse.bass_utils import run_bass_kernel_spmd as _run

    nc = _bacc.Bacc("TRN2", target_bir_lowering=False, num_devices=1, dynamic_dma_scratch_size=1024)
    arrays, args = {}, []
    named = [(name, inputs[name]) for name in _INS] + [("rope_tab", rope_table())]
    for name, value in named:
        a = _np.ascontiguousarray(value)
        arrays[f"in_{name}_dram"] = a
        args.append(nc.dram_tensor(f"in_{name}_dram", a.shape, _mybir.dt.from_np(a.dtype), kind="ExternalInput").ap())
    shape = (1, SEQ, D)
    args.append(nc.dram_tensor("out_0_dram", shape, _mybir.dt.from_np(_np.dtype("float32")), kind="ExternalOutput").ap())
    hybrid_trunk(nc, *args)
    r = _run(nc, [arrays], core_ids=[0])
    return r.results[0]["out_0_dram"]
```

```python
import math
from contextlib import ExitStack, contextmanager

import numpy as np

import concourse.bass as bass
from concourse import mybir
from concourse.alu_op_type import AluOpType as ALU

F32 = mybir.dt.float32
F32R = mybir.dt.float32r
ACT = mybir.ActivationFunctionType
AX = mybir.AxisListType.X
ds = bass.ds

P = 128
SEQ, D, DEPTH = 256, 2048, 2
NT = SEQ // P
KT = D // P
A_HEADS, A_QK, A_V = 4, 64, 128
B_HEADS, B_DIM = 4, 128
I_HEADS, I_DIM = 8, 64
C_HEADS, C_NOPE, C_ROPE, C_V, C_RANK = 8, 128, 64, 128, 512
C_QK = C_NOPE + C_ROPE
TOPK = min(256, SEQ // 4)
THETA = 500000.0
EPS = 1e-6
D_FF = ((8 * D + 3 * 256 - 1) // (3 * 256)) * 256

W_COLS = [2 * A_HEADS * A_QK, 2 * A_HEADS * A_QK, A_HEADS * A_V, B_HEADS * B_DIM, B_DIM, B_DIM,
          I_HEADS * I_DIM, I_DIM, I_HEADS, C_HEADS * C_QK, C_RANK, C_ROPE]
AQ, AK, AV, BQ, BK, BV, IQ, IK, IW, CQ, CKV, CKR, GATES = [sum(W_COLS[:n]) for n in range(len(W_COLS) + 1)]

N = 512
KU = 2
RING = 4
UB = 8
PC = GATES // 10
PROJ1, PROJ2 = 6, 4
NG = 3 * D // N
NC = D // N
NF = D_FF // N
B_A = PROJ1 + PROJ2
B_KV = B_A + A_HEADS
B_C = B_KV + 1
B_BR = B_C + C_HEADS
B_OUT = B_BR + NC
B_FF = B_OUT + NC
B_DN = B_FF + 2 * NF
BLOCKS = B_DN + NF
assert PC * 10 == GATES and PC <= N and C_HEADS + A_HEADS == NG and NF % 2 == 1

G_A, G_KV, G_C, ACT_GROUPS = B_A, B_A + A_HEADS, B_A + A_HEADS + NC, B_A + NG + NC
V_OUT, V_FF, V_DN, DVE_GROUPS = 3 * NC, 4 * NC, 4 * NC + 2 * NF, 5 * NC + 2 * NF
CREDIT = 3

KEYS = 3 * P
SEG = [(0, P), (P, 3 * P)]
NEG = -3e38
TAKEN = float(np.float32(-3.4e38))

ROT = {"a": A_QK // 4, "b": B_DIM // 4, "c": C_ROPE}
ROPE_AT = {"a": 0, "b": 2 * ROT["a"], "c": 2 * (ROT["a"] + ROT["b"])}
ROPE_W = 2 * sum(ROT.values())

GAINS = [("a_q_norm", A_QK), ("a_q_norm", A_QK), ("a_k_norm", A_QK), ("a_k_norm", A_QK), ("a_sub_norm", A_V),
         ("b_q_norm", B_DIM), ("b_k_norm", B_DIM), ("idx_k_norm", I_DIM), ("c_q_norm", C_QK), ("c_k_norm", C_QK)]
GA, _, _, _, GSUB, GBQ, GBK, GIK, GCQ, GCK, G_W = [sum(w for _, w in GAINS[:n]) for n in range(len(GAINS) + 1)]


def rope_table():
    pos = np.arange(SEQ, dtype=np.float32)
    out = []
    for rot in ROT.values():
        half = rot // 2
        inv = (np.float32(THETA) ** (-np.arange(half, dtype=np.float32) * np.float32(2.0) / np.float32(rot)))
        ang = pos[:, None] * inv.astype(np.float32)[None, :]
        out += [np.cos(ang), np.cos(ang), -np.sin(ang), np.sin(ang)]
    return np.concatenate(out, axis=1).astype(np.float32)


class Steps:

    def __init__(self, eng, sem, mark):
        self.eng, self.sem, self.mark, self.base, self.n = eng, sem, mark, 0, 0

    def hold(self):
        self.eng.sem_inc(self.mark, 1)

    def __call__(self, ins, wait=True):
        self.n += 1
        ins.then_inc(self.sem, 1)
        if wait:
            self.eng.wait_ge(self.sem, self.base + self.n)

    @contextmanager
    def turn(self, i, count, stride):
        base, n = self.base, self.n
        self.base, self.n = base + n + i * stride, 0
        yield
        assert 0 < self.n < stride, (self.n, stride)
        self.eng.sem_inc(self.sem, stride - self.n)
        self.base, self.n = base, n + count * stride


def hybrid_trunk(nc, x, attn_norm, w_in, a_q_norm, a_k_norm, a_lambda, a_sub_norm, b_q_norm, b_k_norm,
                 idx_k_norm, c_q_norm, c_kv_norm, w_kv_b, c_k_norm, w_branch, w_out, ffn_norm,
                 w_gate_up, w_down, rope_tab, out):
    gain_of = dict(a_q_norm=a_q_norm, a_k_norm=a_k_norm, a_sub_norm=a_sub_norm, b_q_norm=b_q_norm,
                   b_k_norm=b_k_norm, idx_k_norm=idx_k_norm, c_q_norm=c_q_norm, c_k_norm=c_k_norm)
    gate_store = nc.dram_tensor("gate_store", (DEPTH * NG, P, NT * N), F32, kind="Internal").ap()

    with ExitStack() as ctx:
        def sb(name, shape, dt=F32):
            return ctx.enter_context(nc.sbuf_tensor(name, shape, dt))

        def sem(name):
            return ctx.enter_context(nc.semaphore(name))

        acc = ctx.enter_context(nc.psum_tensor("acc", [P, 8, 512], F32))

        xs = sb("xs", [P, NT, D])
        opa = [sb("opa_hi", [P, KT, SEQ], F32R), sb("opa_lo", [P, KT, SEQ], F32R)]
        opb = [sb("opb_hi", [P, KT, SEQ], F32R), sb("opb_lo", [P, KT, SEQ], F32R)]
        raw = sb("w_raw", [P, RING, KU, N])
        w_hi = sb("w_hi", [P, RING, KU, N], F32R)
        w_lo = sb("w_lo", [P, RING, KU, N], F32R)
        arena = sb("arena", [P, NT * (GATES + C_HEADS * (C_NOPE + C_V))])
        nat = sb("nat", [P, NT, N])
        tmp = sb("tmp", [P, 1024])
        small = sb("small", [P, 4096])
        score_i = sb("score_i", [P, KEYS])
        rope_sb = sb("rope_sb", [P, NT, ROPE_W])
        gains = sb("gains", [P, G_W])
        ident = sb("ident", [P, P])
        causal = sb("causal", [P, KEYS])
        gcol = sb("gcol", [P, 72])
        gnow = sb("gnow", [P, 2 * KT + 4])
        stats = sb("stats", [P, 48])
        xsq = sb("xsq", [P, NT, NC])
        rs = sb("rs", [P, 96])
        rx = sb("rx", [P, 4])
        root_sb = sb("root_sb", [P, 48])
        lam = sb("lam", [P, 8])
        laminit = sb("laminit", [P, DEPTH, 2])
        iws = sb("iws", [P, NT, I_HEADS])
        top8 = sb("top8", [P, NT, 8])
        nmax = sb("nmax", [P, 2, NT])
        sums = sb("sums", [P, 2, NT])
        rsum = sb("rsum", [P, 2, NT])
        krot = sb("krot", [P, NT, C_ROPE])
        rck = sb("rck", [P, NT, C_HEADS])

        proj = arena[:, 0:NT * GATES].rearrange("p (t n) -> p t n", t=NT)
        kv = arena[:, NT * GATES:].rearrange("p (t h n) -> p t h n", t=NT, h=C_HEADS)
        kv_rows = arena[:, NT * GATES:].rearrange("p (t n) -> p t n", t=NT)
        gates = arena[:, A_HEADS * A_V:A_HEADS * A_V + 13 * NT * N].rearrange("p (k n) -> p k n", n=NT * N)
        BRANCH_ORDER = (1, 2, 0)
        FIRST_PIECES = (0, 1, 5)
        hid_t = arena[:, 0:4 * NF * SEQ].rearrange("p (k s) -> p k s", k=4 * NF)
        lamb = small[:, 3840:4096].rearrange("p (f d) -> p f d", f=4)

        def part(a, n):
            return small[:, a:a + n]

        q_rows = part(0, NT * C_QK).rearrange("p (t n) -> p t n", t=NT)
        k_rows = part(384, NT * C_QK).rearrange("p (t n) -> p t n", t=NT)
        v_rows = part(768, NT * C_V).rearrange("p (t n) -> p t n", t=NT)
        qk_rows = part(0, 2 * NT * P).rearrange("p (m t n) -> p m t n", m=2, t=NT)
        bq_rows = part(1024, NT * P).rearrange("p (t n) -> p t n", t=NT)
        ik_rows = part(768, NT * P).rearrange("p (t n) -> p t n", t=NT)
        q_t = small[:, 1280:1792]
        k_t = small[:, 1792:2304]
        s_sb = part(2304, 2 * KEYS).rearrange("p (m n) -> p m n", m=2)
        e_sb = part(3072, 2 * KEYS).rearrange("p (m n) -> p m n", m=2)
        bk_t = sb("bk_t", [P, SEQ])
        bq_t = tmp[:, 768:1024]
        p_t = sb("p_t", [P, 2, KEYS])
        t_row = part(0, NT * N).rearrange("p (t n) -> p t n", t=NT)
        sg = part(1024, NT * N).rearrange("p (t n) -> p t n", t=NT)
        gg = part(2048, NT * N).rearrange("p (t n) -> p t n", t=NT)

        raw_landed = [sem(f"raw_landed{s}") for s in range(RING)]
        hi_ready, unit_done = sem("hi_ready"), sem("unit_done")
        lo_ready = [sem("lo_even"), sem("lo_odd")]
        act_emptied, dve_emptied = sem("act_emptied"), sem("dve_emptied")
        const_landed, gains_landed = sem("const_landed"), sem("gains_landed")
        stored = [sem(f"stored{j}") for j in range(NC)]
        x_ready = [sem(f"x_ready{j}") for j in range(NC)]
        rope_landed = sem("rope_landed")
        pool_const, gcol_t, gains_free = sem("pool_const"), sem("gcol_t"), sem("gains_free")
        dve_step, dve_mark = sem("dve_step"), sem("dve_mark")
        var_ready, root_ready = sem("var_ready"), sem("root_ready")
        rx_ready, rs_ready = sem("rx_ready"), sem("rs_ready")
        gnow_ready = sem("gnow_ready")
        x_t, x_hi, x_lo = sem("x_t"), sem("x_hi"), sem("x_lo")
        m_rows, m_t, m_hi, m_lo = sem("m_rows"), sem("m_t"), sem("m_hi"), sem("m_lo")
        ckv_t, ckv_hi, ckv_lo = sem("ckv_t"), sem("ckv_hi"), sem("ckv_lo")
        ao_rows, ao_t, ao_hi, ao_lo = sem("ao_rows"), sem("ao_t"), sem("ao_hi"), sem("ao_lo")
        i_staged, i_t, i_sb, i_scored, i_relu, i_summed = (sem("i_staged"), sem("i_t"), sem("i_sb"),
                                                           sem("i_scored"), sem("i_relu"), sem("i_summed"))
        lam_dots, lam_exp = sem("lam_dots"), sem("lam_exp")
        head = {h: {n: sem(f"{h}_{n}") for n in ("staged", "qk_t", "qk_sb", "scored", "maxed", "exped", "p_ready",
                                                  "p_t", "p_sb", "o_done", "o_hi", "o_out")} for h in "abc"}
        gate_saved = sem("gate_saved")
        gate_back = [sem(f"gate_back{r}") for r in range(3)]
        gate_open = sem("gate_open")
        sig_ready, h_t, h_sb, jit_hi, jit_lo = (sem("sig_ready"), sem("h_t"), sem("h_sb"), sem("jit_hi"), sem("jit_lo"))

        block = ctx.enter_context(nc.Block())

        def units(l, blk):
            return l * (BLOCKS * UB) + blk * UB

        def lo_count(n, m):
            return n + (m // 2 * 2 + 2 + RING)

        def bank(pair, t=None, n=N):
            return acc[:, 2 * pair:2 * pair + 2, 0:n] if t is None else acc[:, 2 * pair + t, 0:n]

        @block.sync
        def _(sp):
            def weights(w, k_units):
                return w.rearrange("l (u k p) n -> p (l u) k n", k=KU, p=P), k_units

            win, wkv, wbr, wout, wgu, wdn = (weights(w_in, UB), weights(w_kv_b, 2), weights(w_branch, UB),
                                             weights(w_out, UB), weights(w_gate_up, UB), weights(w_down, 2 * NF))

            def unit(n, m, w, l, u, col, width=N):
                slot = m % RING
                sp.wait_ge(lo_ready[m % 2], lo_count(n, m - RING))
                view, per = w
                sp.dma_start(raw[:, slot:slot + 1, :, 0:width],
                             view[:, ds(l * per + u, 1), :, ds(col, width)]).then_inc(raw_landed[slot], 16)

            with sp.Fori(0, DEPTH) as l:
                with sp.Fori(0, PROJ1) as c:
                    n = sp.snap(units(l, 0) + c * UB)
                    for m in range(UB):
                        unit(n, m, win, l, m, c * PC, PC)
                with sp.Fori(0, PROJ2) as c:
                    n = sp.snap(units(l, PROJ1) + c * UB)
                    for m in range(UB):
                        unit(n, m, win, l, m, (PROJ1 + PROJ2 - 1) * PC - c * PC, PC)
                with sp.Fori(0, A_HEADS) as c:
                    n = sp.snap(units(l, B_A) + c * UB)
                    for m in range(UB):
                        unit(n, m, win, l, m, GATES + c * N)
                for m in range(UB):
                    unit(units(l, B_KV), m, wkv, l, m % 2, (m // 2) * N)
                with sp.Fori(0, C_HEADS) as c:
                    n = sp.snap(units(l, B_C) + c * UB)
                    for m in range(UB):
                        unit(n, m, win, l, m, GATES + A_HEADS * N + c * N)
                with sp.Fori(0, NC) as c:
                    n = sp.snap(units(l, B_BR) + c * UB)
                    for m, u in enumerate((2, 3, 4, 5, 6, 7, 0, 1)):
                        unit(n, m, wbr, l, u, c * N)
                with sp.Fori(0, NC) as c:
                    n = sp.snap(units(l, B_OUT) + c * UB)
                    for m in range(UB):
                        unit(n, m, wout, l, m, c * N)
                with sp.Fori(0, NF) as c:
                    n = sp.snap(units(l, B_FF) + c * (2 * UB))
                    for m in range(2 * UB):
                        unit(n, m, wgu, l, m % UB, c * N + (m // UB) * D_FF)
                with sp.Fori(0, NF) as c:
                    n = sp.snap(units(l, B_DN) + c * UB)
                    for m in range(UB):
                        unit(n, m, wdn, l, c * 2 + m % 2, (m // 2) * N)

            out_rows = out.rearrange("a (t p) n -> p (a t) n", p=P)
            for j in range(NC):
                sp.wait_ge(x_ready[j], 16 * (DEPTH + 1))
                sp.dma_start(out_rows[:, :, j * N:(j + 1) * N], xs[:, :, j * N:(j + 1) * N]).then_inc(stored[j], 16)
            for j in range(NC):
                sp.wait_ge(stored[j], 16)

        @block.gpsimd
        def _(pool):
            pool.memset(ident[:, :], 0.0).then_inc(pool_const, 1)
            pool.memset(causal[:, :], 0.0).then_inc(pool_const, 1)
            pool.memset(raw[:, :, :, PC:N], 0.0).then_inc(pool_const, 1)
            for parity in range(2):
                pool.sem_inc(lo_ready[parity], RING)
            pool.wait_ge(pool_const, 3)
            pool.affine_select(out=ident[:, :], in_=ident[:, :], compare_op=ALU.not_equal, fill=1.0, base=0,
                               pattern=[[-1, P]], channel_multiplier=1).then_inc(pool_const, 1)
            for b in (0, 2):
                d = causal[:, b * P:(b + 1) * P]
                pool.affine_select(out=d, in_=d, compare_op=ALU.is_ge, fill=NEG, base=0,
                                   pattern=[[-1, P]], channel_multiplier=1).then_inc(pool_const, 1)

            with pool.Fori(0, DEPTH * BLOCKS) as b:
                n = pool.snap(b * UB)
                for m in range(0, UB, 2):
                    s = m % RING
                    pool.wait_ge(hi_ready, n + (m + 1))
                    pool.tensor_tensor(w_lo[:, s], raw[:, s], w_hi[:, s].bitcast(F32), ALU.subtract).then_inc(lo_ready[0], 2)

        @block.tensor
        def _(pe):
            def unit(n, m, op, kt, pair, first, last, width=N):
                s = m % RING
                pe.wait_ge(lo_ready[m % 2], lo_count(n, m))
                passes = [(op[0], w_hi), (op[0], w_lo), (op[1], w_hi)]
                for k in range(KU):
                    for t in range(NT):
                        for j, (a, w) in enumerate(passes):
                            mm = pe.matmul(bank(pair, t, width), a[:, kt + k, t * P:(t + 1) * P], w[:, s, k, 0:width],
                                           start=(first and k == 0 and j == 0), stop=(last and k == KU - 1 and j == 2))
                mm.then_inc(unit_done, 1)

            def whole(n, m0, op, pair, after, width=N, need=None):
                for m in range(UB):
                    if need:
                        need(m)
                    unit(n, m0 + m, op, KU * m, pair, m == 0, m == UB - 1, width)
                    if m in after:
                        after[m]()

            def rows_to_cols(b0, rows, tiles=4):
                for k in range(tiles):
                    for t in range(NT):
                        at = k * SEQ + t * P
                        mm = pe.transpose(acc[:, b0 + at // 512, at % 512:at % 512 + P],
                                          rows[:, t, k * P:(k + 1) * P], ident[:, :])
                return mm

            def scores(out, q, k, done):
                for j in range(len(q)):
                    pe.matmul(out[:, 0:P], q[j][:, 0:P], k[j][:, 0:P], start=(j == 0), stop=(j == len(q) - 1))
                for j in range(len(q)):
                    mm = pe.matmul(out[:, P:KEYS], q[j][:, P:SEQ], k[j], start=(j == 0), stop=(j == len(q) - 1))
                if done is not None:
                    mm.then_inc(done, 1)

            def probs_t(b, e, done):
                for j in range(3):
                    mm = pe.transpose(acc[:, b, j * P:(j + 1) * P], e[:, j * P:(j + 1) * P], ident[:, :])
                mm.then_inc(done, 1)

            def out_t(b, v, pt, done):
                pe.matmul(acc[:, b, 0:SEQ], v[:, 0], pt[:, 0:SEQ], start=True, stop=False)
                pe.matmul(acc[:, b, P:SEQ], v[:, 1], pt[:, SEQ:KEYS], start=False, stop=True).then_inc(done, 1)

            pe.wait_ge(pool_const, 6)
            pe.wait_ge(const_landed, 16 * 3)
            pe.transpose(acc[:, 7, 0:72], small[0:72, 0:P], ident[0:72, 0:72]).then_inc(gcol_t, 1)
            pe.sem_inc(unit_done, RING)

            with pe.Fori(0, DEPTH) as l:
                for j in range(NC):
                    pe.wait_ge(x_ready[j], l * 16 + 16)
                    if j == NC - 1:
                        pe.wait_ge(gnow_ready, 1)
                    rows_to_cols(2 * j, xs[:, :, j * N:(j + 1) * N]).then_inc(x_t, 1)

                def need_x(m):
                    if m % 2 == 0:
                        pe.wait_ge(x_lo, l * (2 * NC) + (m // 2 + 1))

                with pe.Fori(0, PROJ1 // 2) as i:
                    n = pe.snap(units(l, 0) + i * (2 * UB))
                    g = pe.snap(l * ACT_GROUPS + i * 2)
                    for e in range(2):
                        pe.wait_ge(act_emptied, g + (e + 1))
                        whole(n, e * UB, opa, e, {}, PC, need_x)

                for i in range(PROJ2 // 2):
                    n = units(l, PROJ1 + i * 2)
                    g = l * ACT_GROUPS + PROJ1 + i * 2
                    h = l * PROJ2 + i * 2
                    for e in range(2):
                        pe.wait_ge(act_emptied, g + (e + 1))
                        last = i * 2 + e == PROJ2 - 1

                        def ckv_cols():
                            pe.wait_ge(act_emptied, l * ACT_GROUPS + (2 + PROJ1 + 2))
                            pe.wait_ge(i_sb, h + e)
                            rows_to_cols(4, proj[:, :, CKV:CKV + C_RANK]).then_inc(ckv_t, 1)

                        def pair_t():
                            pe.wait_ge(i_staged, h + (e + 1))
                            if last:
                                pe.wait_ge(ckv_lo, l + 1)
                            for t in range(NT):
                                pe.transpose(acc[:, 4, t * P:(t + 1) * P], bq_rows[:, t], ident[:, :])
                                pe.transpose(acc[:, 4, SEQ + t * P:SEQ + (t + 1) * P], ik_rows[:, t], ident[:, :])
                                mm = pe.transpose(acc[:, 5, t * P:(t + 1) * P], proj[:, t, BK:BK + P], ident[:, :])
                            mm.then_inc(i_t, 1)

                        def pair_scores():
                            pe.wait_ge(i_sb, h + (e + 1))
                            for m in range(2):
                                r = slice(64 * m, 64 * m + 64)
                                scores(acc[:, 6 + m, 0:KEYS], [q_t[r, 0:SEQ]], [q_t[r, SEQ:2 * SEQ]],
                                       i_scored if m else None)

                        whole(n, e * UB, opa, e, {4: pair_t, 5: pair_scores} | ({1: ckv_cols} if last else {}), PC)

                A = head["a"]
                with pe.Fori(0, A_HEADS // 2) as i:
                    n = pe.snap(units(l, B_A) + i * (2 * UB))
                    g = pe.snap(l * ACT_GROUPS + G_A + i * 2)
                    h = pe.snap(l * A_HEADS + i * 2)
                    for e in range(2):
                        pe.wait_ge(act_emptied, g + (e + 1))

                        def a_t():
                            pe.wait_ge(A["staged"], h + (e + 1))
                            for m in range(2):
                                for t in range(NT):
                                    mm = pe.transpose(acc[:, 4, m * SEQ + t * P:m * SEQ + (t + 1) * P],
                                                      qk_rows[:, m, t], ident[:, :])
                            mm.then_inc(A["qk_t"], 1)

                        def a_scores():
                            pe.wait_ge(A["qk_sb"], h + (e + 1))
                            for m in range(2):
                                r = slice(64 * m, 64 * m + 64)
                                scores(acc[:, 5 + m, 0:KEYS], [q_t[r, 0:SEQ]], [q_t[r, SEQ:2 * SEQ]],
                                       A["scored"] if m else None)

                        def a_p_t():
                            pe.wait_ge(A["p_ready"], h + (e + 1))
                            probs_t(4, e_sb[:, 0], A["p_t"])

                        def a_out():
                            pe.wait_ge(A["p_sb"], h + (e + 1))
                            pe.wait_ge(A["o_out"], h + (e + 1))
                            pt = p_t[:, 0]
                            pe.matmul(acc[:, 7, 0:P], pt[:, 0:P], v_rows[:, 0], start=True, stop=True)
                            pe.matmul(acc[:, 7, P:SEQ], pt[:, P:SEQ], v_rows[:, 0], start=True, stop=False)
                            pe.matmul(acc[:, 7, P:SEQ], pt[:, SEQ:KEYS], v_rows[:, 1], start=False,
                                      stop=True).then_inc(A["o_done"], 1)

                        whole(n, e * UB, opa, e, {1: a_t, 2: a_scores, 5: a_p_t, 6: a_out})

                n = units(l, B_KV)
                for j in range(NC):
                    pe.wait_ge(act_emptied, l * ACT_GROUPS + (G_KV + j + 1))
                    if j == NC - 1:
                        pe.wait_ge(A["o_out"], (l + 1) * A_HEADS + 1)
                    for u in range(2):
                        unit(n, 2 * j + u, opb, KU * u, j % 2, u == 0, u == 1)

                B, C = head["b"], head["c"]
                with pe.Fori(0, C_HEADS // 2) as i:
                    n = pe.snap(units(l, B_C) + i * (2 * UB))
                    g = pe.snap(l * ACT_GROUPS + G_C + i * 2)
                    h = pe.snap(l * C_HEADS + i * 2)
                    hb = pe.snap(l * B_HEADS + i)
                    for e in range(2):
                        pe.wait_ge(act_emptied, g + (e + 1))

                        def c_t():
                            pe.wait_ge(C["staged"], h + (e + 1))
                            if e == 1:
                                pe.wait_ge(B["p_ready"], hb + 1)
                            half = C_QK // 2
                            for b, rows in ((4, q_rows), (5, k_rows)):
                                for j in range(2):
                                    for t in range(NT):
                                        mm = pe.transpose(acc[0:half, b, j * SEQ + t * P:j * SEQ + (t + 1) * P],
                                                          rows[:, t, j * half:(j + 1) * half], ident[:, :])
                            mm.then_inc(C["qk_t"], 1)

                        def c_scores():
                            pe.wait_ge(C["qk_sb"], h + (e + 1))
                            half = C_QK // 2
                            scores(acc[:, 6, 0:KEYS], [q_t[0:half, j * SEQ:(j + 1) * SEQ] for j in range(2)],
                                   [k_t[0:half, j * SEQ:(j + 1) * SEQ] for j in range(2)], C["scored"])

                        def c_p_t():
                            pe.wait_ge(C["p_ready"], h + (e + 1))
                            probs_t(4, e_sb[:, 0], C["p_t"])

                        def c_out():
                            pe.wait_ge(C["p_sb"], h + (e + 1))
                            pe.wait_ge(C["o_out"], h + (e + 1))
                            out_t(7, v_rows, p_t[:, 0], C["o_done"])

                        def b_t():
                            pe.wait_ge(B["staged"], hb + 1)
                            for t in range(NT):
                                mm = pe.transpose(acc[:, 5, t * P:(t + 1) * P], bq_rows[:, t], ident[:, :])
                            mm.then_inc(B["qk_t"], 1)

                        def b_scores():
                            pe.wait_ge(B["qk_sb"], hb + 1)
                            scores(acc[:, 5, 0:KEYS], [bq_t[:, :]], [bk_t[:, :]], B["scored"])

                        def b_p_t():
                            probs_t(5, e_sb[:, 1], B["p_t"])

                        def b_out():
                            pe.wait_ge(B["p_sb"], hb + 1)
                            out_t(5, proj[:, :, BV:BV + P], p_t[:, 1], B["o_done"])

                        after = {2: c_t, 3: c_scores, 6: c_p_t, 7: c_out}
                        after.update({4: b_t, 5: b_scores} if e == 0 else {4: b_p_t, 5: b_out})
                        if e == 0:
                            pe.wait_ge(B["o_out"], hb + 1)
                        whole(n, e * UB, opa, e, after)

                def branches(n, j, after):
                    for r, (pair, k0, us) in enumerate(((0, 4, (0, 1)), (3, 8, (2, 3, 4, 5)), (1, 0, (6, 7)))):
                        pe.wait_ge(dve_emptied, l * DVE_GROUPS + j * 3 + (r + 1))
                        if after is first_chunk:
                            if r == 0:
                                pe.wait_ge(act_emptied, l * ACT_GROUPS + (ACT_GROUPS - 1 + 2))
                                pe.wait_ge(B["o_out"], (l + 1) * B_HEADS + 1)
                            if r == 2:
                                pe.wait_ge(act_emptied, (l + 1) * ACT_GROUPS + 2)
                                pe.wait_ge(ao_lo, l + 1)
                            if r == 1:
                                pe.wait_ge(C["o_out"], (l + 1) * C_HEADS + 1)
                        for u in us:
                            unit(n, u, opb, k0 + KU * (u - us[0]), pair, u == us[0], u == us[-1])
                            if u in after:
                                after[u]()

                def ao_cols():
                    pe.wait_ge(ao_rows, l + 1)
                    rows_to_cols(4, proj[:, :, 0:A_HEADS * A_V]).then_inc(ao_t, 1)

                first_chunk = {2: ao_cols}
                branches(units(l, B_BR), 0, first_chunk)
                with pe.Fori(1, NC) as j:
                    n = pe.snap(units(l, B_BR) + j * UB)

                    def merged_rolled():
                        pe.wait_ge(m_rows, l * NC + j)
                        pe.wait_ge(m_lo, l * NC + j)
                        rows_to_cols(4, nat).then_inc(m_t, 1)

                    branches(n, j, {1: merged_rolled})

                def x_cols(j):
                    pe.wait_ge(dve_emptied, l * DVE_GROUPS + (CREDIT + V_OUT + j + 1))
                    pe.wait_ge(x_lo, l * (2 * NC) + (NC + j))
                    rows_to_cols(4, xs[:, :, j * N:(j + 1) * N]).then_inc(x_t, 1)

                for j in range(NC):
                    pe.wait_ge(dve_emptied, l * DVE_GROUPS + (CREDIT + (V_OUT - 3 + j if j < 2 else V_OUT + j - 2) + 1))

                    def last_merged():
                        pe.wait_ge(m_rows, l * NC + NC)
                        pe.wait_ge(m_lo, l * NC + NC)
                        rows_to_cols(4, nat).then_inc(m_t, 1)

                    def need_m(m):
                        if j == 0 and m == 6:
                            pe.wait_ge(m_lo, l * NC + NC + 1)
                        if j == 0 and m == 0:
                            pe.wait_ge(m_lo, l * NC + NC)

                    def next_x():
                        if j == 1:
                            pe.wait_ge(m_lo, l * NC + NC + 1)
                        x_cols(j - 1)

                    whole(units(l, B_OUT + j), 0, opa, j % 2, {1: last_merged} if j == 0 else {1: next_x}, N, need_m)

                def hidden_t(j):
                    pe.wait_ge(dve_emptied, l * DVE_GROUPS + (j * 2 + (CREDIT + V_FF + 2)))
                    pe.wait_ge(h_sb, l * NF + j + 1)
                    rows_to_cols(4, nat).then_inc(h_t, 1)

                def need_ff(m):
                    if m == 0:
                        pe.wait_ge(x_lo, l * (2 * NC) + (2 * NC - 1))
                    if m == 6:
                        pe.wait_ge(x_lo, l * (2 * NC) + 2 * NC)

                for e in range(2):
                    pe.wait_ge(dve_emptied, l * DVE_GROUPS + (CREDIT + V_FF + e - 1))
                    whole(units(l, B_FF), e * UB, opb, e, {1: lambda: x_cols(NC - 1)} if e == 0 else {}, N,
                          need_ff if e == 0 else None)
                with pe.Fori(1, NF) as j:
                    n = pe.snap(units(l, B_FF) + j * (2 * UB))
                    for e in range(2):
                        pe.wait_ge(dve_emptied, l * DVE_GROUPS + j * 2 + (CREDIT + V_FF + e - 1))
                        if e == 0:
                            whole(n, 0, opb, 0, {1: lambda: hidden_t(j - 1)})
                        else:
                            whole(n, UB, opb, 1, {})

                def down(n, m0, kk, value, first, last, after={}):
                    pe.wait_ge(jit_lo, value)
                    for c in range(NC):
                        if first and c < 2:
                            pe.wait_ge(dve_emptied, l * DVE_GROUPS + (CREDIT + V_DN + c - 1))
                        if first and c == 2:
                            pe.wait_ge(h_sb, l * NF + (NF + 1))
                        for u in range(2):
                            unit(n, m0 + 2 * c + u, opa, 4 * (kk % 2) + KU * u, c, first and u == 0, last and u == 1)
                            if 2 * c + u in after:
                                after[2 * c + u]()

                down(units(l, B_DN), 0, 0, l * NF + 1, True, False, {1: lambda: hidden_t(NF - 1)})
                with pe.Fori(0, (NF - 3) // 2) as i:
                    n = pe.snap(units(l, B_DN + 1) + i * (2 * UB))
                    for e in range(2):
                        down(n, e * UB, 1 + e, l * NF + i * 2 + (e + 2), False, False)
                for e in range(2):
                    down(units(l, BLOCKS - 2 + e), 0, 1 + e, l * NF + (NF - 1 + e), False, e == 1)

        @block.scalar
        def _(act):
            def copy(out, in_, scale=1.0):
                return act.activation(out, in_, ACT.Copy, scale=scale)

            def hi(n, nq, m):
                s = m % RING
                act.wait_ge(raw_landed[s], nq + 16 * (m // RING + 1))
                act.wait_ge(unit_done, n + (m + 1))
                copy(w_hi[:, s], raw[:, s]).then_inc(hi_ready, 1)

            def through(n, nq, m0, after, units_=UB):
                for m in range(UB):
                    if m < units_:
                        hi(n, nq, m0 + m + RING)
                    if m in after:
                        after[m](n)

            def bases(l, blk, i=None, per=1):
                n, q = units(l, blk), l * (BLOCKS * UB * 4) + blk * UB * 4
                if i is None:
                    return n, q
                return act.snap(n + i * (per * UB)), act.snap(q + i * (per * UB * 4))

            def done(n, m):
                act.wait_ge(unit_done, n + (RING + m + 1))

            def root(value, v, r):
                act.wait_ge(var_ready, value)
                act.activation(r, v, ACT.Sqrt).then_inc(root_ready, 1)

            def split_hi(value, t_sem, dst, b0, gain, h_sem):
                act.wait_ge(t_sem, value)
                src = acc[:, b0:b0 + 2, :].rearrange("p b (k s) -> p (b k) s", s=SEQ)
                if gain is None:
                    copy(dst, src).then_inc(h_sem, 1)
                    return
                for k in range(4):
                    ins = copy(dst[:, k], src[:, k], gain[:, k:k + 1])
                ins.then_inc(h_sem, 1)

            def load_gains(l):
                at = 0
                for name, width in GAINS:
                    act.dma_start(gains[:, at:at + width],
                                  gain_of[name][ds(l, 1), :].to_broadcast([P, width])).then_inc(gains_landed, 16)
                    at += width
                act.dma_start(lamb, a_lambda.rearrange("l f d -> l (f d)")[ds(l, 1), :].to_broadcast([P, 4 * A_QK])
                              .rearrange("p (f d) -> p f d", f=4)).then_inc(gains_landed, 16)

            row = 0
            for g in (attn_norm, ffn_norm, c_kv_norm):
                rows = g.rearrange("l (k p) -> (l k) p", p=P)
                act.dma_start(small[row:row + rows.shape[0], 0:P], rows).then_inc(const_landed, 16)
                row += rows.shape[0]
            x_rows = x.rearrange("a (t p) n -> p (a t) n", p=P)
            for j in range(NC):
                act.dma_start(xs[:, :, j * N:(j + 1) * N], x_rows[:, :, j * N:(j + 1) * N]).then_inc(x_ready[j], 16)
            act.dma_start(rope_sb[:, :, :], rope_tab.rearrange("(t p) n -> p t n", p=P)).then_inc(rope_landed, 16)
            act.sem_inc(act_emptied, 2)
            act.wait_ge(pool_const, 6)
            act.sem_inc(m_lo, 1)
            act.sem_inc(h_sb, 1)

            with act.Fori(0, DEPTH) as l:
                n, nq = bases(l, 0)
                for j in range(NC):
                    hi(n, nq, j)
                    if j == 0:
                        act.wait_ge(gnow_ready, l + 1)
                    split_hi(l * (2 * NC) + (j + 1), x_t, opa[0][:, 4 * j:4 * j + 4], 2 * j,
                             gnow[:, 4 * j:4 * j + 4], x_hi)
                act.wait_ge(gains_free, l + 1)
                load_gains(l)

                def leave_proj(n, m, pair, col):
                    done(n, m)
                    act.wait_ge(rx_ready, l * 2 + 1)
                    for t in range(NT):
                        ins = copy(proj[:, t, ds(col, PC)], bank(pair, t, PC), rx[:, t:t + 1])
                    ins.then_inc(act_emptied, 1)

                through(n, nq, 0, {5: lambda n: root(l * 4 + 1, stats[:, 0:2], root_sb[:, 0:2]),
                                   7: lambda n: leave_proj(n, 7, 0, 0)})
                through(n, nq, UB, {7: lambda n: leave_proj(n, UB + 7, 1, PC)})
                with act.Fori(1, PROJ1 // 2) as i:
                    n, nq = bases(l, 0, i, 2)
                    for e in range(2):
                        through(n, nq, e * UB, {7: lambda n: leave_proj(n, e * UB + 7, e, i * (2 * PC) + e * PC)})

                root(l * 4 + 2, stats[:, 0:44], root_sb[:, 0:44])
                for i in range(PROJ2 // 2):
                    n, nq = bases(l, PROJ1 + i * 2)
                    h = l * PROJ2 + i * 2
                    for e in range(2):
                        def pair_sb(n):
                            act.wait_ge(i_t, h + (e + 1))
                            copy(q_t, acc[:, 4, :])
                            copy(bk_t[:, :], acc[:, 5, 0:SEQ]).then_inc(i_sb, 1)

                        def pair_relu(n):
                            act.wait_ge(i_scored, h + (e + 1))
                            act.wait_ge(i_summed, h + (e + 1))
                            act.activation(s_sb, acc[:, 6:8, 0:KEYS], ACT.Relu).then_inc(i_relu, 1)

                        def leave(n):
                            leave_proj(n, e * UB + 7, e, (PROJ1 + PROJ2 - 1) * PC - e * PC - i * (2 * PC))

                        def ckv_split(n):
                            split_hi(l + 1, ckv_t, opb[0][:, 0:4], 4, gnow[:, 2 * KT:2 * KT + 4], ckv_hi)

                        through(n, nq, e * UB, {4: pair_sb, 6: pair_relu, 7: leave} |
                                ({1: ckv_split} if i * 2 + e == PROJ2 - 1 else {}))

                act.wait_ge(lam_dots, l + 1)
                act.activation(lam[:, 2:4], lam[:, 0:2], ACT.Exp).then_inc(lam_exp, 1)

                def save_gate(n, m, e, value, chunk, saved):
                    done(n, m)
                    act.wait_ge(gate_saved, saved)
                    for t in range(NT):
                        ins = copy(nat[:, t], bank(e, t), rx[:, t:t + 1])
                    ins.then_inc(act_emptied, 1)
                    act.wait_ge(act_emptied, value)
                    act.dma_start(gate_store[ds(chunk, 1)].rearrange("a p n -> p (a n)"),
                                  nat.rearrange("p t n -> p (t n)")).then_inc(gate_saved, 16)

                def exps(S, value, maps):
                    act.wait_ge(S["maxed"], value)
                    for m in maps:
                        for t, (a, b) in enumerate(SEG):
                            ins = act.activation(e_sb[:, m, a:b], s_sb[:, m, a:b], ACT.Exp, bias=nmax[:, m, t:t + 1],
                                                 accum_out=sums[:, m, t:t + 1])
                    ins.then_inc(S["exped"], 1)

                A, B, C = head["a"], head["b"], head["c"]
                with act.Fori(0, A_HEADS // 2) as i:
                    n, nq = bases(l, B_A, i, 2)
                    h = act.snap(l * A_HEADS + i * 2)
                    for e in range(2):
                        def a_qk_sb(n):
                            act.wait_ge(A["qk_t"], h + (e + 1))
                            copy(q_t, acc[:, 4, :]).then_inc(A["qk_sb"], 1)

                        def a_p_sb(n):
                            act.wait_ge(A["p_t"], h + (e + 1))
                            copy(p_t[:, 0], acc[:, 4, 0:KEYS]).then_inc(A["p_sb"], 1)

                        def a_o(n):
                            act.wait_ge(A["o_done"], h + (e + 1))
                            copy(proj[:, :, ds(AQ + i * (2 * A_V) + e * A_V, A_V)],
                                 acc[:, 7, 0:SEQ].rearrange("p (t n) -> p t n", t=NT)).then_inc(A["o_out"], 1)

                        def leave(n):
                            save_gate(n, e * UB + 7, e, l * ACT_GROUPS + i * 2 + (2 + G_A + e + 1),
                                      l * NG + i * 2 + e, l * (NG * 16) + i * 32 + (16 * e + 16))

                        def a_o_leave(n):
                            a_o(n)
                            leave(n)

                        through(n, nq, e * UB, {1: a_qk_sb, 3: lambda n: exps(A, h + (e + 1), (0, 1)),
                                                5: a_p_sb, 7: a_o_leave})

                n, nq = bases(l, B_KV)

                def leave_kv(m):
                    j = m // 2
                    done(n, m)
                    copy(kv_rows[:, :, j * N:(j + 1) * N], bank(j % 2)).then_inc(act_emptied, 1)

                through(n, nq, 0, {m: (lambda n, m=m: leave_kv(m)) for m in (1, 3, 5, 7)})

                def c_turn(i, first):
                    n, nq = bases(l, B_C, i, 2)
                    h = act.snap(l * C_HEADS + i * 2)
                    hb = act.snap(l * B_HEADS + i)
                    for e in range(2):
                        def c_qk_sb(n):
                            act.wait_ge(C["qk_t"], h + (e + 1))
                            half = C_QK // 2
                            copy(q_t[0:half, :], acc[0:half, 4, :])
                            copy(k_t[0:half, :], acc[0:half, 5, :]).then_inc(C["qk_sb"], 1)

                        def c_exps(n):
                            exps(C, h + (e + 1), (0,))

                        def b_sb(n):
                            if e == 0:
                                act.wait_ge(B["qk_t"], hb + 1)
                                copy(bq_t[:, :], acc[:, 5, 0:SEQ]).then_inc(B["qk_sb"], 1)
                            else:
                                act.wait_ge(B["p_t"], hb + 1)
                                copy(p_t[:, 1], acc[:, 5, 0:KEYS]).then_inc(B["p_sb"], 1)

                        def c_p_sb(n):
                            act.wait_ge(C["p_t"], h + (e + 1))
                            copy(p_t[:, 0], acc[:, 4, 0:KEYS]).then_inc(C["p_sb"], 1)

                        def b_exps(n):
                            exps(B, hb + 1, (1,))

                        def b_o(n):
                            act.wait_ge(B["o_done"], hb + 1)
                            copy(opb[0][:, ds(i + A_HEADS, 1), :].rearrange("p a s -> p (a s)"),
                                 acc[:, 5, 0:SEQ]).then_inc(B["o_hi"], 1)

                        def c_o(n):
                            act.wait_ge(C["o_done"], h + (e + 1))
                            copy(opb[0][:, ds(i * 2 + (A_HEADS + B_HEADS + e), 1), :].rearrange("p a s -> p (a s)"),
                                 acc[:, 7, 0:SEQ]).then_inc(C["o_hi"], 1)

                        def leave(n):
                            save_gate(n, e * UB + 7, e, l * ACT_GROUPS + i * 2 + (2 + G_C + e + 1),
                                      l * NG + i * 2 + (A_HEADS + e), l * (NG * 16) + i * 32 + (16 * (A_HEADS + e) + 16))

                        def exps_sb(n):
                            c_exps(n)
                            b_sb(n)

                        def p_b(n):
                            c_p_sb(n)
                            if e == 0:
                                b_exps(n)

                        def leave_o(n):
                            leave(n)
                            c_o(n)

                        after = {2: c_qk_sb, 4: exps_sb, 6: p_b, 7: leave_o}
                        if e == 1:
                            after[5] = b_o
                        if first and e == 0:
                            after[0] = lambda n: root(l * 4 + 3, stats[:, 0:42], root_sb[:, 0:42])
                        through(n, nq, e * UB, after)

                c_turn(0, True)
                with act.Fori(1, C_HEADS // 2) as i:
                    c_turn(i, False)

                def load_gate(r, piece, j):
                    act.dma_start(gates[:, ds(piece, 1)].rearrange("p k n -> p (k n)"),
                                  gate_store[ds(l * NG + BRANCH_ORDER[r] * NC + j, 1)].rearrange("a p n -> p (a n)"))\
                        .then_inc(gate_back[r], 16)

                def open_piece(r):
                    act.wait_ge(gate_back[r], l * (NC * 16) + 16)
                    g = gates[:, FIRST_PIECES[r]]
                    act.activation(g, g, ACT.Sigmoid).then_inc(gate_open, 1)

                def open_chunk(j):
                    for r in range(3):
                        act.wait_ge(gate_back[r], l * (NC * 16) + j * 16 + 16)
                    g = gates[:, ds(4 * j - 2, 3)].rearrange("p k n -> p (k n)")
                    act.activation(g, g, ACT.Sigmoid).then_inc(gate_open, 3)

                def merged_hi(value, j):
                    split_hi(value, m_t, opa[0][:, ds(j * 4, 4)], 4, None, m_hi)

                def load_c(n):
                    act.wait_ge(C["o_out"], (l + 1) * C_HEADS + 1)
                    load_gate(1, FIRST_PIECES[1], 0)

                def all_saved(n):
                    act.wait_ge(gate_saved, (l + 1) * (NG * 16) + 16)
                    open_piece(0)

                def ao_and_load(n):
                    split_hi(l + 1, ao_t, opb[0][:, 0:4], 4, None, ao_hi)
                    load_gate(0, 2, 1)

                def open_and_load_1(n):
                    open_piece(1)
                    load_gate(1, 3, 1)

                def open_and_load_2(n):
                    open_piece(2)
                    load_gate(2, 4, 1)

                load_gate(0, FIRST_PIECES[0], 0)
                load_gate(2, FIRST_PIECES[2], 0)
                n, nq = bases(l, B_BR)
                through(n, nq, 0, {0: load_c, 1: all_saved, 2: ao_and_load, 4: open_and_load_1, 5: open_and_load_2})
                with act.Fori(1, NC - 1) as j:
                    n, nq = bases(l, B_BR, j)

                    def open_and_load(n):
                        open_chunk(j)
                        load_gate(0, 4 * j + 2, j + 1)

                    through(n, nq, 0, {1: lambda n: merged_hi(l * NC + j, j - 1), 2: open_and_load,
                                       4: lambda n: load_gate(1, 4 * j + 3, j + 1),
                                       6: lambda n: load_gate(2, 4 * j + 4, j + 1)})
                n, nq = bases(l, B_OUT - 1)
                through(n, nq, 0, {1: lambda n: merged_hi(l * NC + NC - 1, NC - 2), 3: lambda n: open_chunk(NC - 1)})

                def x_hi_of(j):
                    split_hi(l * (2 * NC) + (NC + j + 1), x_t, opb[0][:, 4 * j:4 * j + 4], 4,
                             gnow[:, KT + 4 * j:KT + 4 * j + 4], x_hi)

                for j in range(NC):
                    n, nq = bases(l, B_OUT + j)
                    through(n, nq, 0, {1: (lambda n: merged_hi(l * NC + NC, NC - 1)) if j == 0 else
                                       (lambda n: x_hi_of(j - 1))})

                def sigmoids(n, m, value):
                    done(n, m)
                    act.wait_ge(dve_emptied, value)
                    for t in range(NT):
                        ins = act.activation(sg[:, t], bank(0, t), ACT.Sigmoid, scale=rx[:, 2 + t:3 + t])
                    ins.then_inc(sig_ready, 1)

                def hidden_sb(value, j):
                    act.wait_ge(h_t, value)
                    copy(hid_t[:, ds(j * 4, 4)], acc[:, 4:6, :].rearrange("p b (k s) -> p (b k) s", s=SEQ))\
                        .then_inc(h_sb, 1)

                n, nq = bases(l, B_FF)

                def first_ffn(n):
                    root(l * 4 + 4, stats[:, 0:2], root_sb[:, 0:2])

                def first_sig(n):
                    act.wait_ge(rx_ready, l * 2 + 2)
                    sigmoids(n, UB - 1, l * DVE_GROUPS + (CREDIT + V_FF))

                through(n, nq, 0, {1: lambda n: x_hi_of(NC - 1), 4: first_ffn, 7: first_sig})
                through(n, nq, UB, {})
                with act.Fori(1, NF - 1) as j:
                    n, nq = bases(l, B_FF, j, 2)
                    through(n, nq, 0, {1: lambda n: hidden_sb(l * NF + j, j - 1),
                                       7: lambda n: sigmoids(n, UB - 1, l * DVE_GROUPS + j * 2 + (CREDIT + V_FF))})
                    through(n, nq, UB, {})

                def jit(value, kk, slot):
                    act.wait_ge(h_sb, value)
                    copy(opa[0][:, 4 * slot:4 * slot + 4], hid_t[:, ds(kk * 4, 4)]).then_inc(jit_hi, 1)

                n, nq = bases(l, B_FF + 2 * (NF - 1))
                through(n, nq, 0, {1: lambda n: hidden_sb(l * NF + NF - 1, NF - 2), 4: lambda n: jit(l * NF + 2, 0, 0),
                                   7: lambda n: sigmoids(n, UB - 1, l * DVE_GROUPS + (2 * (NF - 1) + CREDIT + V_FF))})
                n, nq = bases(l, B_DN - 1)
                through(n, nq, 0, {4: lambda n: jit(l * NF + 3, 1, 1)})
                n, nq = bases(l, B_DN)
                through(n, nq, 0, {1: lambda n: hidden_sb(l * NF + NF, NF - 1)})
                with act.Fori(0, (NF - 3) // 2) as i:
                    n, nq = bases(l, B_DN + 1, i, 2)
                    for e in range(2):
                        through(n, nq, e * UB, {1: lambda n: jit(l * NF + i * 2 + (e + 4), i * 2 + (e + 2), e)})
                n, nq = bases(l, BLOCKS - 2)
                through(n, nq, 0, {1: lambda n: jit(l * NF + (NF + 1), NF - 1, 0)})
                n, nq = bases(l, BLOCKS - 1)
                through(n, nq, 0, {}, UB - RING)

        @block.vector
        def _(dve):
            step = Steps(dve, dve_step, dve_mark)

            def wait(s, v):
                dve.wait_ge(s, v)

            def tt(out, a, b, op):
                return dve.tensor_tensor(out, a, b, op)

            def bc(ap, n):
                return ap.unsqueeze(3).to_broadcast([P, ap.shape[1], ap.shape[2], n])

            def over(ap, h):
                return ap.unsqueeze(2).to_broadcast([P, ap.shape[1], h, ap.shape[2]])

            def gain(at, d, h):
                return gains[:, at:at + d].unsqueeze(1).unsqueeze(1).to_broadcast([P, NT, h, d])

            def heads(ap, h):
                return ap.rearrange("p t (h d) -> p t h d", h=h)

            def squares(src, dst):
                h, d = src.shape[2], src.shape[3]
                v = tmp[:, 0:NT * h * d].rearrange("p (t h d) -> p t h d", t=NT, h=h)
                step(tt(v, src, src, ALU.mult))
                step(dve.tensor_reduce(dst, v, AX, ALU.add))

            def rope(X, h, rot, at):
                half = rot // 2
                ta = tmp[:, 0:NT * h * rot].rearrange("p (t h d) -> p t h d", t=NT, h=h)
                tb = tmp[:, 512:512 + NT * h * rot].rearrange("p (t h d) -> p t h d", t=NT, h=h)
                cc, ss = rope_sb[:, :, at:at + rot], rope_sb[:, :, at + rot:at + 2 * rot]
                step(tt(ta, X[:, :, :, 0:rot], over(cc, h), ALU.mult), False)
                step(tt(tb[:, :, :, 0:half], X[:, :, :, half:rot], over(ss[:, :, 0:half], h), ALU.mult), False)
                step(tt(tb[:, :, :, half:rot], X[:, :, :, 0:half], over(ss[:, :, half:rot], h), ALU.mult))
                step(tt(X[:, :, :, 0:rot], ta, tb, ALU.add))

            def mean(a, b, d):
                return dve.tensor_scalar(stats[:, a:b], stats[:, a:b], 1.0 / d, EPS, ALU.mult, ALU.add)

            def reciprocal_roots(value, n, out, ready):
                v, r, y, z = stats[:, 0:n], root_sb[:, 0:n], tmp[:, 0:n], tmp[:, 64:64 + n]
                wait(root_ready, value)
                step(dve.reciprocal(y, r))
                step(tt(z, v, y, ALU.mult))
                step(tt(z, z, y, ALU.mult))
                step(dve.tensor_scalar(z, z, -0.5, 1.5, ALU.mult, ALU.add))
                tt(out, y, z, ALU.mult).then_inc(ready, 1)

            def chunk_squares(j):
                v = tmp[:, 0:NT * N].rearrange("p (t n) -> p t n", t=NT)
                c = xs[:, :, j * N:(j + 1) * N]
                step(tt(v, c, c, ALU.mult))
                step(dve.tensor_reduce(xsq[:, :, j], v, AX, ALU.add))

            def row_factors(l, which, value):
                step(dve.tensor_reduce(stats[:, 0:NT], xsq[:, :, :], AX, ALU.add))
                mean(0, NT, D).then_inc(var_ready, 1)
                wait(var_ready, value)
                reciprocal_roots(value, NT, rx[:, 2 * which:2 * which + 2], rx_ready)
                wait(rx_ready, l * 2 + which + 1)

            def split_lo(value, h_sem, hi_, lo_, b0, gain_, l_sem):
                wait(h_sem, value)
                src = acc[:, b0:b0 + 2, :].rearrange("p b (k s) -> p (b k) s", s=SEQ)
                if gain_ is None:
                    tt(lo_, src, hi_.bitcast(F32), ALU.subtract).then_inc(l_sem, 1)
                    return
                for k in range(4):
                    ins = dve.scalar_tensor_tensor(lo_[:, k], src[:, k], gain_[:, k:k + 1], hi_[:, k].bitcast(F32),
                                                   ALU.mult, ALU.subtract)
                ins.then_inc(l_sem, 1)

            def softmax_in(S, value, b0, maps, scale, mask):
                m0, m1 = maps[0], maps[-1] + 1
                k = m1 - m0
                wait(S["scored"], value)
                step(dve.scalar_tensor_tensor(s_sb[:, m0:m1], acc[:, b0:b0 + k, 0:KEYS], scale,
                                              mask.unsqueeze(1).to_broadcast([P, k, KEYS]), ALU.mult, ALU.add))
                for t, (a, b) in enumerate(SEG):
                    ins = dve.tensor_reduce(nmax[:, m0:m1, t], s_sb[:, m0:m1, a:b], AX, ALU.max, negate=True)
                    if t == 0:
                        step(ins, False)
                ins.then_inc(S["maxed"], 1)

            def softmax_out(S, value, m):
                wait(S["exped"], value)
                step(dve.reciprocal(rsum[:, m], sums[:, m]))
                for t, (a, b) in enumerate(SEG):
                    ins = dve.tensor_scalar(e_sb[:, m, a:b], e_sb[:, m, a:b], rsum[:, m, t:t + 1], None, ALU.mult)
                    if t == 0:
                        step(ins, False)
                ins.then_inc(S["p_ready"], 1)

            def lo(n, m):
                s = m % RING
                wait(hi_ready, n + (m + 1))
                tt(w_lo[:, s], raw[:, s], w_hi[:, s].bitcast(F32), ALU.subtract).then_inc(lo_ready[1], 2)

            def through(n, m0, after, units_=UB):
                for m in range(UB):
                    if m % 2 == 1 and m < units_:
                        lo(n, m0 + m + RING)
                    for f in after.get(m, ()):
                        f()

            for l_ in range(DEPTH):
                init = 0.8 - 0.6 * math.exp(-0.3 * l_)
                step(dve.memset(laminit[:, l_, 0:1], init), False)
                step(dve.memset(laminit[:, l_, 1:2], 1.0 - init))
            dve.sem_inc(dve_emptied, CREDIT)
            dve.sem_inc(gains_free, 1)
            dve.sem_inc(i_summed, 1)
            dve.sem_inc(head["a"]["o_out"], 1)
            dve.sem_inc(head["b"]["o_out"], 1)
            dve.sem_inc(head["c"]["o_out"], 1)
            dve.sem_inc(gate_saved, 16)
            wait(gcol_t, 1)
            step(dve.tensor_copy(gcol[:, :], acc[:, 7, 0:72]))
            dve.tensor_copy(gnow[:, 0:KT], gcol[:, 0:KT]).then_inc(gnow_ready, 1)
            wait(pool_const, 6)

            LAYER = 1500
            step.hold()
            with dve.Fori(0, DEPTH) as l, step.turn(l, DEPTH, LAYER):
                A, B, C = head["a"], head["b"], head["c"]
                step(dve.tensor_copy(gnow[:, KT:2 * KT], gcol[:, ds(l * KT + DEPTH * KT, KT)]), False)
                step(dve.tensor_copy(gnow[:, 2 * KT:], gcol[:, ds(l * 4 + 2 * DEPTH * KT, 4)]))
                for j in range(NC):
                    split_lo(l * (2 * NC) + (j + 1), x_hi, opa[0][:, 4 * j:4 * j + 4], opa[1][:, 4 * j:4 * j + 4],
                             2 * j, gnow[:, 4 * j:4 * j + 4], x_lo)
                    if j in (0, 2):
                        lo(units(l, 0), j + 1)

                def lambdas():
                    wait(gains_landed, (l + 1) * (16 * (len(GAINS) + 1)))
                    wait(rope_landed, 16)
                    dots = tmp[:, 0:2 * A_QK].rearrange("p (f d) -> p f d", f=2)
                    step(tt(dots, lamb[:, 0::2], lamb[:, 1::2], ALU.mult))
                    dve.tensor_reduce(lam[:, 0:2], dots, AX, ALU.add).then_inc(lam_dots, 1)
                    step(dve.tensor_scalar(gains[:, GSUB:GSUB + A_V], gains[:, GSUB:GSUB + A_V],
                                           laminit[:, ds(l, 1), 1:2].rearrange("p a b -> p (a b)"), None, ALU.mult))

                def projected(block):
                    wait(act_emptied, l * ACT_GROUPS + (2 + block + 1))

                s_a = stats[:, 0:32].rearrange("p (t h) -> p t h", t=NT)

                def projected_squares(col, src, h, dst):
                    projected(col // PC)
                    squares(heads(src, h), dst)

                through(units(l, 0), 0, {j: [lambda j=j: chunk_squares(j)] for j in range(NC)} |
                        {5: [lambda: row_factors(l, 0, l * 4 + 1)]})
                through(units(l, 1), 0, {0: [lambdas]})
                through(units(l, 2), 0, {1: [lambda: projected_squares(AK, proj[:, :, AQ:AK], 8, s_a[:, :, 0:8])]})
                through(units(l, 3), 0, {1: [lambda: projected_squares(AV, proj[:, :, AK:AV], 8, s_a[:, :, 8:16])]})
                through(units(l, 4), 0, {})
                through(units(l, 5), 0, {
                    1: [lambda: projected_squares(BK, proj[:, :, BQ:BK], 4, stats[:, 34:42].rearrange("p (t h) -> p t h", t=NT)),
                        lambda: projected_squares(BV, proj[:, :, BK:BV], 1, stats[:, 42:44].rearrange("p (t h) -> p t h", t=NT))]})
                projected(PROJ1 - 1)
                squares(heads(proj[:, :, IK:IW], 1), stats[:, 32:34].rearrange("p (t h) -> p t h", t=NT))
                step(mean(0, 34, A_QK))
                mean(34, 44, B_DIM).then_inc(var_ready, 1)
                wait(var_ready, l * 4 + 2)
                reciprocal_roots(l * 4 + 2, 44, rs[:, 0:44], rs_ready)
                wait(rs_ready, l * 2 + 1)
                r_a = rs[:, 0:32].rearrange("p (t h) -> p t h", t=NT)
                r_ik = rs[:, 32:34].rearrange("p (t h) -> p t h", t=NT)
                r_bq = rs[:, 34:42].rearrange("p (t h) -> p t h", t=NT)
                r_bk = rs[:, 42:44].rearrange("p (t h) -> p t h", t=NT)

                def normed(X, h, d, r, g, rot, at):
                    step(tt(X, X, bc(r, d), ALU.mult))
                    step(tt(X, X, g, ALU.mult))
                    rope(X, h, rot, at)

                def index_rows():
                    normed(heads(proj[:, :, IK:IW], 1), 1, I_DIM, r_ik, gain(GIK, I_DIM, 1), ROT["a"], ROPE_AT["a"])
                    for m in range(2):
                        step(dve.tensor_copy(ik_rows[:, :, m * I_DIM:(m + 1) * I_DIM], proj[:, :, IK:IW]), False)
                    rope(heads(proj[:, :, IQ:IK], I_HEADS), I_HEADS, ROT["a"], ROPE_AT["a"])

                def index_weights():
                    step(dve.tensor_scalar(iws[:, :, :], proj[:, :, IW:IW + I_HEADS], I_HEADS ** -0.5 * I_DIM ** -0.5,
                                           None, ALU.mult), False)
                    step(dve.memset(score_i[:, :], 0.0))

                def norm_bk():
                    normed(heads(proj[:, :, BK:BV], 1), 1, B_DIM, r_bk, gain(GBK, B_DIM, 1), ROT["b"], ROPE_AT["b"])

                for i in range(PROJ2):
                    n = units(l, PROJ1 + i)

                    def stage_pair():
                        dve.tensor_copy(bq_rows, proj[:, :, ds(IQ + i * P, P)]).then_inc(i_staged, 1)

                    def norm_a():
                        a4 = heads(proj[:, :, ds(AQ + i * (4 * A_QK), 4 * A_QK)], 4)
                        g4 = gains[:, ds(GA + i * A_QK, A_QK)].unsqueeze(1).unsqueeze(1).to_broadcast([P, NT, 4, A_QK])
                        normed(a4, 4, A_QK, r_a[:, :, ds(i * 4, 4)], g4, ROT["a"], ROPE_AT["a"])

                    def norm_b():
                        b1 = heads(proj[:, :, ds(BQ + i * B_DIM, B_DIM)], 1)
                        normed(b1, 1, B_DIM, r_bq[:, :, ds(i, 1)], gain(GBQ, B_DIM, 1), ROT["b"], ROPE_AT["b"])

                    def pair_sums():
                        wait(i_relu, l * PROJ2 + i + 1)
                        for m in range(2):
                            for t, (a, b) in enumerate(SEG):
                                ins = dve.scalar_tensor_tensor(score_i[:, a:b], s_sb[:, m, a:b],
                                                               iws[:, t, ds(i * 2 + m, 1)], score_i[:, a:b],
                                                               ALU.mult, ALU.add)
                                if (m, t) != (1, 1):
                                    step(ins, (m, t) == (0, 1))
                        ins.then_inc(i_summed, 1)
                        wait(i_summed, l * PROJ2 + i + 2)

                    def ckv_split():
                        split_lo(l + 1, ckv_hi, opb[0][:, 0:4], opb[1][:, 0:4], 4, gnow[:, 2 * KT:2 * KT + 4], ckv_lo)

                    after = {0: [stage_pair], 2: [norm_a], 3: [norm_b], 7: [pair_sums]}
                    if i == 0:
                        after[0] = [index_rows, norm_bk, stage_pair, index_weights]
                    if i == PROJ2 - 1:
                        after[1] = [ckv_split]
                    through(n, 0, after)

                step(tt(score_i[:, :], score_i[:, :], causal[:, :], ALU.add))
                wait(lam_exp, l + 1)
                step(tt(lam[:, 4:5], lam[:, 2:3], lam[:, 3:4], ALU.subtract))
                step(dve.tensor_scalar(lam[:, 5:6], lam[:, 4:5], laminit[:, ds(l, 1), 0:1].rearrange("p a b -> p (a b)"),
                                       None, ALU.add))

                r_cq = stats[:, 0:16].rearrange("p (t h) -> p t h", t=NT)
                step.hold()
                with dve.Fori(0, A_HEADS) as i, step.turn(i, A_HEADS, 64):
                    h = l * A_HEADS + i
                    n = dve.snap(units(l, B_A) + i * UB)

                    def stage_a():
                        wait(A["o_out"], h + 1)
                        for m, at in enumerate((AQ, AK)):
                            step(dve.tensor_copy(qk_rows[:, m], proj[:, :, ds(at + i * P, P)]), False)
                        dve.tensor_copy(v_rows, proj[:, :, ds(AV + i * P, P)]).then_inc(A["staged"], 1)

                    def cq_squares():
                        squares(heads(proj[:, :, ds(CQ + i * (2 * C_QK), 2 * C_QK)], 2), r_cq[:, :, ds(i * 2, 2)])

                    def a_in():
                        softmax_in(A, h + 1, 5, (0, 1), A_QK ** -0.5, causal[:, :])

                    def a_probs():
                        wait(A["exped"], h + 1)
                        step(dve.reciprocal(rsum[:, :, :], sums[:, :, :]))
                        step(dve.tensor_scalar(rsum[:, 1], rsum[:, 1], lam[:, 5:6], None, ALU.mult))
                        for t, (a, b) in enumerate(SEG):
                            step(dve.tensor_scalar(e_sb[:, 1, a:b], e_sb[:, 1, a:b], rsum[:, 1, t:t + 1], None, ALU.mult), t == 1)
                        for t, (a, b) in enumerate(SEG):
                            ins = dve.scalar_tensor_tensor(e_sb[:, 0, a:b], e_sb[:, 0, a:b], rsum[:, 0, t:t + 1],
                                                           e_sb[:, 1, a:b], ALU.mult, ALU.subtract)
                            if t == 0:
                                step(ins, False)
                        ins.then_inc(A["p_ready"], 1)

                    def take_8():
                        step.hold()
                        for t, (a, b) in enumerate(SEG):
                            step(dve.max(top8[:, t], score_i[:, a:b]), t == 1)
                        step.hold()
                        for t, (a, b) in enumerate(SEG):
                            step(dve.match_replace(score_i[:, a:b], top8[:, t], score_i[:, a:b], TAKEN), t == 1)

                    rounds = TOPK // 8 // A_HEADS
                    assert rounds == 2
                    through(n, 0, {0: [stage_a, cq_squares], 2: [a_in], 4: [a_probs], 5: [take_8], 6: [take_8]})

                s_ck = stats[:, 16:32].rearrange("p (t h) -> p t h", t=NT)
                kr = krot[:, :, :].unsqueeze(2)

                def mask():
                    step(dve.tensor_scalar(score_i[:, :], score_i[:, :], TAKEN, NEG, ALU.not_equal, ALU.mult))
                    step(tt(score_i[:, :], score_i[:, :], causal[:, :], ALU.min))

                def ao_squares():
                    wait(A["o_out"], (l + 1) * A_HEADS + 1)
                    squares(heads(proj[:, :, 0:A_HEADS * A_V], A_HEADS), stats[:, 32:40].rearrange("p (t h) -> p t h", t=NT))

                def latent_squares():
                    squares(heads(proj[:, :, CKV:CKR], 1), stats[:, 40:42].rearrange("p (t h) -> p t h", t=NT))
                    squares(heads(proj[:, :, CKR:GATES], 1), stats[:, 42:44].rearrange("p (t h) -> p t h", t=NT))

                def means():
                    step(mean(0, 16, C_QK), False)
                    step(mean(32, 40, A_V), False)
                    step(mean(40, 42, C_RANK))
                    step(dve.reciprocal(stats[:, 44:46], stats[:, 40:42]))

                def shared_k():
                    step(tt(kr, heads(proj[:, :, CKR:GATES], 1), gain(GCK, C_ROPE, 1), ALU.mult))
                    rope(kr, 1, C_ROPE, ROPE_AT["c"])

                def k_squares(j):
                    wait(act_emptied, l * ACT_GROUPS + (2 + G_KV + j + 1))
                    squares(kv[:, :, 2 * j:2 * j + 2, 0:C_NOPE], s_ck[:, :, 2 * j:2 * j + 2])

                through(units(l, B_KV), 0, {0: [mask, ao_squares], 1: [latent_squares], 2: [means, shared_k],
                                            4: [lambda: k_squares(0)], 5: [lambda: k_squares(1)], 6: [lambda: k_squares(2)],
                                            7: [lambda: k_squares(3)]})
                step(tt(s_ck, s_ck, stats[:, 44:46].unsqueeze(2).to_broadcast([P, NT, C_HEADS]), ALU.mult))
                step(tt(s_ck, s_ck, stats[:, 42:44].unsqueeze(2).to_broadcast([P, NT, C_HEADS]), ALU.add))
                mean(16, 32, C_QK).then_inc(var_ready, 1)
                wait(var_ready, l * 4 + 3)
                reciprocal_roots(l * 4 + 3, 42, rs[:, 48:90], rs_ready)
                wait(rs_ready, l * 2 + 2)
                r_cq2 = rs[:, 48:64].rearrange("p (t h) -> p t h", t=NT)
                r_ck = rs[:, 64:80].rearrange("p (t h) -> p t h", t=NT)
                r_ao = rs[:, 80:88].rearrange("p (t h) -> p t h", t=NT)
                r_kv = rs[:, 88:90]
                step(tt(rck[:, :, :], r_ck, r_kv.unsqueeze(2).to_broadcast([P, NT, C_HEADS]), ALU.mult))

                step.hold()
                with dve.Fori(0, C_HEADS // 2) as i, step.turn(i, C_HEADS // 2, 64):
                    h = l * C_HEADS + i * 2
                    hb = l * B_HEADS + i

                    def stage_c(e):
                        j = i * 2 + e
                        wait(C["o_out"], h + (e + 1))
                        q4, k4 = q_rows.unsqueeze(2), k_rows.unsqueeze(2)
                        step(tt(q4, heads(proj[:, :, ds(CQ + i * (2 * C_QK) + e * C_QK, C_QK)], 1),
                                bc(r_cq2[:, :, ds(j, 1)], C_QK), ALU.mult))
                        step(tt(k4[:, :, :, 0:C_ROPE], krot[:, :, :].unsqueeze(2), bc(r_ck[:, :, ds(j, 1)], C_ROPE), ALU.mult), False)
                        step(tt(k4[:, :, :, C_ROPE:], kv[:, :, ds(j, 1), 0:C_NOPE], bc(rck[:, :, ds(j, 1)], C_NOPE), ALU.mult), False)
                        step(tt(v_rows.unsqueeze(2), kv[:, :, ds(j, 1), C_NOPE:], bc(r_kv.unsqueeze(2), C_V), ALU.mult), False)
                        step(tt(q4, q4, gain(GCQ, C_QK, 1), ALU.mult))
                        rope(q4, 1, C_ROPE, ROPE_AT["c"])
                        tt(k4[:, :, :, C_ROPE:], k4[:, :, :, C_ROPE:], gain(GCK + C_ROPE, C_NOPE, 1), ALU.mult)\
                            .then_inc(C["staged"], 1)

                    def out_lo(S, value, b, kt):
                        wait(S["o_hi"], value)
                        at = ds(kt, 1)
                        tt(opb[1][:, at, :], acc[:, b:b + 1, 0:SEQ], opb[0][:, at, :].bitcast(F32), ALU.subtract)\
                            .then_inc(S["o_out"], 1)

                    def stage_b():
                        dve.tensor_copy(bq_rows, proj[:, :, ds(BQ + i * B_DIM, B_DIM)]).then_inc(B["staged"], 1)

                    def c_in(e):
                        softmax_in(C, h + (e + 1), 6, (0,), C_QK ** -0.5, causal[:, :])

                    def c_lo(e):
                        out_lo(C, h + (e + 1), 7, i * 2 + (A_HEADS + B_HEADS + e))

                    n = dve.snap(units(l, B_C) + i * (2 * UB))
                    through(n, 0, {0: [lambda: stage_c(0), stage_b],
                                   3: [lambda: c_in(0)],
                                   5: [lambda: softmax_out(C, h + 1, 0),
                                       lambda: softmax_in(B, hb + 1, 5, (1,), B_DIM ** -0.5, score_i[:, :])],
                                   7: [lambda: softmax_out(B, hb + 1, 1), lambda: c_lo(0)]})
                    through(n, UB, {0: [lambda: stage_c(1)],
                                    3: [lambda: c_in(1)],
                                    5: [lambda: softmax_out(C, h + 2, 0)],
                                    6: [lambda: out_lo(B, hb + 1, 5, i + A_HEADS)],
                                    7: [lambda: c_lo(1)]})

                ao = heads(proj[:, :, 0:A_HEADS * A_V], A_HEADS)
                step(tt(ao, ao, bc(r_ao, A_V), ALU.mult))
                step(tt(ao, ao, gain(GSUB, A_V, A_HEADS), ALU.mult))
                dve.sem_inc(gains_free, 1)
                dve.sem_inc(ao_rows, 1)

                m_ = nat[:, :, :]

                def merge_part(j, n, e0, r, piece):
                    pair, last = ((0, 1), (3, 5), (1, 7))[r]
                    wait(unit_done, n + (RING + last + 1))
                    wait(gate_open, l * (NC * 3) + j * 3 + (r + 1))
                    gate = gates[:, ds(piece, 1)].rearrange("p k (t n) -> p (k t) n", t=NT)
                    tt(t_row if r else m_, bank(pair), gate, ALU.mult).then_inc(dve_emptied, 1)
                    wait(dve_emptied, e0 + (CREDIT + r + 1))
                    if r == 1:
                        step(tt(m_, m_, t_row, ALU.add))
                    if r == 2:
                        tt(m_, m_, t_row, ALU.add).then_inc(m_rows, 1)

                def merged_lo(value, j):
                    split_lo(value, m_hi, opa[0][:, ds(j * 4, 4)], opa[1][:, ds(j * 4, 4)], 4, None, m_lo)

                e0 = l * DVE_GROUPS
                after = {m: [lambda r=r: merge_part(0, units(l, B_BR), e0, r, FIRST_PIECES[r])]
                         for r, m in enumerate((3, 6, 7))}
                after[3].insert(0, lambda: split_lo(l + 1, ao_hi, opb[0][:, 0:4], opb[1][:, 0:4], 4, None, ao_lo))
                through(units(l, B_BR), 0, after)
                with dve.Fori(1, NC) as j, step.turn(j - 1, NC - 1, 16):
                    n = dve.snap(units(l, B_BR) + j * UB)
                    e0 = dve.snap(l * DVE_GROUPS + j * 3)
                    after = {m: [lambda r=r: merge_part(j, n, e0, r, j * 4 + (r - 2))] for r, m in enumerate((3, 5, 7))}
                    after[2] = [lambda: merged_lo(l * NC + j, j - 1)]
                    through(n, 0, after)

                def x_chunk(j):
                    wait(unit_done, units(l, B_OUT + j) + (RING + UB))
                    c = slice(j * N, (j + 1) * N)
                    tt(xs[:, :, c], xs[:, :, c], bank(j % 2), ALU.add).then_inc(dve_emptied, 1)
                    wait(dve_emptied, l * DVE_GROUPS + (CREDIT + V_OUT + j + 1))

                def x_chunk_lo(j):
                    split_lo(l * (2 * NC) + (NC + j + 1), x_hi, opb[0][:, 4 * j:4 * j + 4], opb[1][:, 4 * j:4 * j + 4],
                             4, gnow[:, KT + 4 * j:KT + 4 * j + 4], x_lo)

                for j in range(NC):
                    after = {2: [lambda: merged_lo(l * NC + NC, NC - 1)]} if j == 0 else \
                        {2: [lambda: x_chunk_lo(j - 1)], 3: [lambda: chunk_squares(j - 1)]}
                    after[7] = [lambda: x_chunk(j)]
                    through(units(l, B_OUT + j), 0, after)

                def gate_part(j):
                    wait(sig_ready, l * NF + j + 1)
                    for t in range(NT):
                        ins = dve.scalar_tensor_tensor(gg[:, t], bank(0, t), rx[:, 2 + t:3 + t], sg[:, t],
                                                       ALU.mult, ALU.mult)
                        if t == 0:
                            step(ins, False)
                    ins.then_inc(dve_emptied, 1)
                    wait(dve_emptied, l * DVE_GROUPS + j * 2 + (CREDIT + V_FF + 1))

                def up_part(j, n):
                    wait(unit_done, n + (RING + 2 * UB))
                    wait(h_sb, l * NF + j + 1)
                    for t in range(NT):
                        ins = dve.scalar_tensor_tensor(nat[:, t], bank(1, t), rx[:, 2 + t:3 + t], gg[:, t],
                                                       ALU.mult, ALU.mult)
                        if t == 0:
                            step(ins, False)
                    ins.then_inc(dve_emptied, 1)

                def jit(value, kk, slot):
                    wait(jit_hi, value)
                    s = slice(4 * slot, 4 * slot + 4)
                    tt(opa[1][:, s], hid_t[:, ds(kk * 4, 4)], opa[0][:, s].bitcast(F32), ALU.subtract).then_inc(jit_lo, 1)

                n = units(l, B_FF)
                through(n, 0, {2: [lambda: x_chunk_lo(NC - 1)], 3: [lambda: chunk_squares(NC - 1)],
                               4: [lambda: row_factors(l, 1, l * 4 + 4)]})
                through(n, UB, {1: [lambda: gate_part(0)], 7: [lambda: up_part(0, n)]})
                with dve.Fori(1, NF - 1) as j, step.turn(j - 1, NF - 2, 16):
                    n = dve.snap(units(l, B_FF) + j * (2 * UB))
                    through(n, 0, {})
                    through(n, UB, {1: [lambda: gate_part(j)], 7: [lambda: up_part(j, n)]})
                n = units(l, B_FF + 2 * (NF - 1))
                through(n, 0, {5: [lambda: jit(l * NF + 1, 0, 0)]})
                through(n, UB, {1: [lambda: gate_part(NF - 1)], 5: [lambda: jit(l * NF + 2, 1, 1)],
                                7: [lambda: up_part(NF - 1, n)]})

                through(units(l, B_DN), 0, {
                    3: [lambda: dve.tensor_copy(gnow[:, 0:KT], gcol[:, ds(l * KT + KT, KT)]).then_inc(gnow_ready, 1)]})
                with dve.Fori(0, (NF - 3) // 2) as i:
                    n = dve.snap(units(l, B_DN + 1) + i * (2 * UB))
                    for e in range(2):
                        through(n, e * UB, {2: [lambda: jit(l * NF + i * 2 + (e + 3), i * 2 + (e + 2), e)]})
                through(units(l, BLOCKS - 2), 0, {2: [lambda: jit(l * NF + NF, NF - 1, 0)]})

                def x_done(j):
                    wait(unit_done, units(l, BLOCKS - 1) + (RING + 2 * j + 2))
                    c = slice(j * N, (j + 1) * N)
                    tt(xs[:, :, c], xs[:, :, c], bank(j), ALU.add).then_inc(dve_emptied, 1)
                    wait(dve_emptied, l * DVE_GROUPS + (CREDIT + V_DN + j + 1))
                    dve.sem_inc(x_ready[j], 16)

                through(units(l, BLOCKS - 1), 0, {2 * j + 1: [lambda j=j: x_done(j)] for j in range(NC)}, UB - RING)


_INS = ['x', 'attn_norm', 'w_in', 'a_q_norm', 'a_k_norm', 'a_lambda', 'a_sub_norm', 'b_q_norm', 'b_k_norm',
        'idx_k_norm', 'c_q_norm', 'c_kv_norm', 'w_kv_b', 'c_k_norm', 'w_branch', 'w_out', 'ffn_norm',
        'w_gate_up', 'w_down']


def kernel(**inputs):
    import numpy as _np
    import concourse.bacc as _bacc
    from concourse import mybir as _mybir
    from concourse.bass_utils import run_bass_kernel_spmd as _run

    nc = _bacc.Bacc("TRN2", target_bir_lowering=False, num_devices=1, dynamic_dma_scratch_size=1024)
    arrays, args = {}, []
    named = [(name, inputs[name]) for name in _INS] + [("rope_tab", rope_table())]
    for name, value in named:
        a = _np.ascontiguousarray(value)
        arrays[f"in_{name}_dram"] = a
        args.append(nc.dram_tensor(f"in_{name}_dram", a.shape, _mybir.dt.from_np(a.dtype), kind="ExternalInput").ap())
    shape = (1, SEQ, D)
    args.append(nc.dram_tensor("out_0_dram", shape, _mybir.dt.from_np(_np.dtype("float32")), kind="ExternalOutput").ap())
    hybrid_trunk(nc, *args)
    r = _run(nc, [arrays], core_ids=[0])
    return r.results[0]["out_0_dram"]
```
